# Optimizing a Trainium2 kernel written in Bass

```python
import math
import jax, jax.numpy as jnp
from jax import lax
import numpy as np

D_MODEL = 1024
BATCH = 1
SEQ = 2048
DEPTH = 1
DEC_BATCH = 8
DEC_SEQ = 1
PAST_LEN = 4096
PAGE_SIZE = 128

MIX_WIDTH = D_MODEL
HG_WIDTH = MIX_WIDTH // 2
HG_HEAD_DIM = 128
HG_HEADS = HG_WIDTH // HG_HEAD_DIM
ATT_WIDTH = MIX_WIDTH - HG_WIDTH
ATT_HEAD_DIM = 64
ATT_HEADS = ATT_WIDTH // ATT_HEAD_DIM
ROPE_DIM = ATT_HEAD_DIM // 4
ROPE_THETA = 500000.0
DILATED_PATTERNS = ((128, 1), (512, 4), (2048, 16))
MAX_WINDOW = 2048
HG_CHUNK = 64
N_GROUPS = 8
EXPERTS_PER_GROUP = 8
N_EXPERTS = N_GROUPS * EXPERTS_PER_GROUP
TOP_K_INNER = 2
D_FF_EXPERT = 512
MOE_BLOCK = 128
IN_COLS = 4 * HG_WIDTH + 3 * ATT_WIDTH
RMS_EPS = 1e-6

kernel_name = 'hymba_hgrn2_longnet_hmoe_step'

def rmsnorm(x, g):
    xf = x.astype(jnp.float32)
    y = xf * lax.rsqrt(jnp.mean(xf * xf, axis=-1, keepdims=True) + RMS_EPS)
    return (y * g.astype(jnp.float32)).astype(x.dtype)

def rope_partial(x, pos):
    half = ROPE_DIM // 2
    inv_freq = ROPE_THETA ** (-jnp.arange(half, dtype=jnp.float32) / half)
    ang = pos.astype(jnp.float32)[:, None] * inv_freq[None, :]
    cos = jnp.cos(ang)[None, :, None, :]
    sin = jnp.sin(ang)[None, :, None, :]
    xr = x[..., :ROPE_DIM].astype(jnp.float32)
    x1, x2 = xr[..., :half], xr[..., half:]
    rot = jnp.concatenate([x1 * cos - x2 * sin, x2 * cos + x1 * sin], axis=-1)
    return jnp.concatenate([rot.astype(x.dtype), x[..., ROPE_DIM:]], axis=-1)

def mixer_inputs(h, w_in_l, lb_l, pos):
    B, T, _ = h.shape
    z = h @ w_in_l
    cuts = [HG_WIDTH, 2 * HG_WIDTH, 3 * HG_WIDTH, 4 * HG_WIDTH,
            4 * HG_WIDTH + ATT_WIDTH, 4 * HG_WIDTH + 2 * ATT_WIDTH]
    zq, zf, zi, zg, aq, ak, av = jnp.split(z, cuts, axis=-1)
    hg = lambda a: a.reshape(B, T, HG_HEADS, HG_HEAD_DIM)
    at = lambda a: a.reshape(B, T, ATT_HEADS, ATT_HEAD_DIM)
    f = lb_l + (1.0 - lb_l) * jax.nn.sigmoid(zf.astype(jnp.float32))
    hq = hg(jax.nn.silu(zq.astype(jnp.float32)))
    hk = hg(1.0 - f)
    hv = hg(zi.astype(jnp.float32))
    hlogf = hg(jnp.log(f))
    return hq, hk, hv, hlogf, zg, rope_partial(at(aq), pos), rope_partial(at(ak), pos), at(av)

def hgrn2_recurrence(q, k, v, logf, s0):
    B, T, H, K = q.shape
    V = v.shape[-1]
    c = min(HG_CHUNK, T)
    n = -(-T // c)
    pad = n * c - T
    padf = lambda a: jnp.pad(a, ((0, 0), (0, pad), (0, 0), (0, 0)))
    chunks = lambda a: padf(a).reshape(B, n, c, H, a.shape[-1]).swapaxes(0, 1)
    causal = jnp.tril(jnp.ones((c, c), dtype=bool))[None, :, :, None, None]

    def step(s, inp):
        qc, kc, vc, gc = inp
        b = jnp.cumsum(gc, axis=1)
        diff = b[:, :, None] - b[:, None, :]
        decay = jnp.exp(jnp.where(causal, diff, -jnp.inf))
        a = jnp.einsum('btshk,bshk->bhts', qc[:, :, None] * decay, kc)
        o = (jnp.einsum('bhts,bshv->bthv', a, vc)
             + jnp.einsum('bthk,bhkv->bthv', qc * jnp.exp(b), s))
        b_last = b[:, -1]
        s_new = (jnp.exp(b_last)[..., None] * s
                 + jnp.einsum('bshk,bshv->bhkv', kc * jnp.exp(b_last[:, None] - b), vc))
        return s_new, o

    s_T, o = lax.scan(step, s0.astype(jnp.float32),
                      (chunks(q), chunks(k), chunks(v), chunks(logf)))
    o = o.swapaxes(0, 1).reshape(B, n * c, H, V)[:, :T]
    return o, s_T

def dilated_attention_prompt(q, k, v, window, dil):
    B, T, H, E = q.shape
    n = window // dil
    span = n * dil
    nb = -(-T // span)
    pad = nb * span - T

    def blocks(a):
        a = jnp.pad(a.astype(jnp.float32), ((0, 0), (0, pad), (0, 0), (0, 0)))
        return a.reshape(B, nb, n, dil, H, E)

    qb, kb, vb = blocks(q), blocks(k), blocks(v)
    with_prev = lambda a: jnp.concatenate(
        [jnp.pad(a, ((0, 0), (1, 0), (0, 0), (0, 0), (0, 0), (0, 0)))[:, :-1], a], axis=2)
    kk, vv = with_prev(kb), with_prev(vb)
    s = jnp.einsum('bnirhe,bnjrhe->bnrhij', qb, kk) * (E ** -0.5)
    i = jnp.arange(n)[:, None]
    j = jnp.arange(2 * n)[None, :]
    blk = jnp.arange(nb)[:, None, None]
    steps = i + n - j
    valid = (steps >= 0) & (steps <= n) & (blk * n + j - n >= 0)
    s = jnp.where(valid[None, :, None, None], s, -jnp.inf)
    m = jnp.max(s, axis=-1, keepdims=True)
    p = jnp.exp(s - m)
    den = jnp.sum(p, axis=-1)
    o = jnp.einsum('bnrhij,bnjrhe->bnirhe', p, vv) / jnp.transpose(den, (0, 1, 4, 2, 3))[..., None]
    lse = jnp.transpose(m[..., 0] + jnp.log(den), (0, 1, 4, 2, 3))
    return o.reshape(B, nb * span, H, E)[:, :T], lse.reshape(B, nb * span, H)[:, :T]

def dilated_attention_step(q, k_rows, v_rows, window, dil):
    B, S, H, E = q.shape
    L = k_rows.shape[1] - S
    n = window // dil
    idx = L + jnp.arange(S)[:, None] - dil * jnp.arange(n + 1)[None, :]
    valid = idx >= 0
    idx = jnp.maximum(idx, 0)
    kg = k_rows[:, idx].astype(jnp.float32)
    vg = v_rows[:, idx].astype(jnp.float32)
    s = jnp.einsum('bshe,bsjhe->bshj', q.astype(jnp.float32), kg) * (E ** -0.5)
    s = jnp.where(valid[None, :, None, :], s, -jnp.inf)
    m = jnp.max(s, axis=-1, keepdims=True)
    p = jnp.exp(s - m)
    den = jnp.sum(p, axis=-1)
    o = jnp.einsum('bshj,bsjhe->bshe', p, vg) / den[..., None]
    return o, m[..., 0] + jnp.log(den)

def merge_dilations(outs, lses):
    w = jax.nn.softmax(jnp.stack(lses, axis=0), axis=0)
    return jnp.einsum('pbth,pbthe->bthe', w, jnp.stack(outs, axis=0))

def mixer_output(hg_o, zg, att_o, hg_norm_g_l, w_out_l, dtype):
    B, T = zg.shape[:2]
    g = hg_norm_g_l.reshape(HG_HEADS, HG_HEAD_DIM).astype(jnp.float32)
    hn = hg_o * lax.rsqrt(jnp.mean(hg_o * hg_o, axis=-1, keepdims=True) + RMS_EPS) * g
    hn = hn.reshape(B, T, HG_WIDTH) * jax.nn.silu(zg.astype(jnp.float32))
    cat = jnp.concatenate([hn, att_o.reshape(B, T, ATT_WIDTH)], axis=-1).astype(dtype)
    return cat @ w_out_l

def hier_route(h, w_rg, w_re):
    hf = h.astype(jnp.float32)
    lg = hf @ w_rg.astype(jnp.float32)
    pg = jax.nn.softmax(lg, axis=-1)
    _, gi = lax.top_k(lg, 1)
    p_grp = jnp.take_along_axis(pg, gi, axis=-1)[:, 0]
    le_all = jnp.einsum('td,gde->tge', hf, w_re.astype(jnp.float32))
    le = jnp.take_along_axis(le_all, gi[:, :, None], axis=1)[:, 0]
    tv, ti = lax.top_k(jax.nn.softmax(le, axis=-1), TOP_K_INNER)
    gates = p_grp[:, None] * tv / jnp.sum(tv, axis=-1, keepdims=True)
    return gi * EXPERTS_PER_GROUP + ti, gates

def moe_apply(h, experts, gates, w_g, w_u, w_d):
    T, D = h.shape
    A = T * TOP_K_INNER
    blk = max(1, min(MOE_BLOCK, A // N_EXPERTS))
    nblk = (A + N_EXPERTS * (blk - 1)) // blk + 1
    flat_e = experts.reshape(-1)
    order = jnp.argsort(flat_e)
    e_sorted = flat_e[order]
    tok_sorted = order // TOP_K_INNER
    counts = jnp.zeros((N_EXPERTS,), jnp.int32).at[flat_e].add(1)
    padded = (counts + blk - 1) // blk * blk
    pad_end = jnp.cumsum(padded)
    pad_start = pad_end - padded
    start = jnp.cumsum(counts) - counts
    slot = pad_start[e_sorted] + jnp.arange(A, dtype=jnp.int32) - start[e_sorted]
    slot_tok = jnp.zeros((nblk * blk,), jnp.int32).at[slot].set(tok_sorted)
    blk_expert = jnp.minimum(
        jnp.searchsorted(pad_end, jnp.arange(nblk, dtype=jnp.int32) * blk, side='right'),
        N_EXPERTS - 1)
    xb = h[slot_tok].reshape(nblk, blk, D)

    def run(args):
        xs, e = args
        return (jax.nn.silu(xs @ w_g[e]) * (xs @ w_u[e])) @ w_d[e]

    yb = lax.map(run, (xb, blk_expert)).reshape(nblk * blk, D)
    contrib = (yb[slot].astype(jnp.float32) * gates.reshape(-1)[order][:, None]).astype(h.dtype)
    return jnp.zeros_like(h).at[tok_sorted].add(contrib)

def channel_mixer(h, w_rg, w_re, w_g, w_u, w_d):
    B, T, D = h.shape
    hf = h.reshape(B * T, D)
    experts, gates = hier_route(hf, w_rg, w_re)
    return moe_apply(hf, experts, gates, w_g, w_u, w_d).reshape(B, T, D)

def setup_inputs(seed: int = 0) -> dict:
    key = jax.random.key(seed)
    ks = jax.random.split(key, 17)
    f32 = jnp.float32
    win_rows = min(MAX_WINDOW, PAST_LEN)

    def nrm(k, shape, scale):
        return scale * jax.random.normal(k, shape, f32)

    return {
        'x_prompt': nrm(ks[0], (BATCH, SEQ, D_MODEL), 1.0),
        'x_sample': nrm(ks[1], (DEC_BATCH, DEC_SEQ, D_MODEL), 1.0),
        'cache_attn_k': nrm(ks[2], (DEPTH, DEC_BATCH, win_rows, ATT_HEADS, ATT_HEAD_DIM), 1.0),
        'cache_attn_v': nrm(ks[3], (DEPTH, DEC_BATCH, win_rows, ATT_HEADS, ATT_HEAD_DIM), 1.0),
        'state_hgrn': nrm(ks[4], (DEPTH, DEC_BATCH, HG_HEADS, HG_HEAD_DIM, HG_HEAD_DIM), 0.1),
        'w_in': nrm(ks[5], (DEPTH, D_MODEL, IN_COLS), D_MODEL ** -0.5),
        'w_out': nrm(ks[6], (DEPTH, MIX_WIDTH, D_MODEL), MIX_WIDTH ** -0.5),
        'hg_lb_logits': nrm(ks[7], (DEPTH + 1, HG_WIDTH), 0.5),
        'hg_norm_g': 1.0 + nrm(ks[8], (DEPTH, HG_WIDTH), 0.02),
        'norm_mix_g': 1.0 + nrm(ks[9], (DEPTH, D_MODEL), 0.02),
        'norm_ffn_g': 1.0 + nrm(ks[10], (DEPTH, D_MODEL), 0.02),
        'norm_final_g': 1.0 + nrm(ks[11], (D_MODEL,), 0.02),
        'w_route_group': nrm(ks[12], (DEPTH, D_MODEL, N_GROUPS), D_MODEL ** -0.5),
        'w_route_expert': nrm(ks[13], (DEPTH, N_GROUPS, D_MODEL, EXPERTS_PER_GROUP), D_MODEL ** -0.5),
        'w_expert_gate': nrm(ks[14], (DEPTH, N_EXPERTS, D_MODEL, D_FF_EXPERT), D_MODEL ** -0.5),
        'w_expert_up': nrm(ks[15], (DEPTH, N_EXPERTS, D_MODEL, D_FF_EXPERT), D_MODEL ** -0.5),
        'w_expert_down': nrm(ks[16], (DEPTH, N_EXPERTS, D_FF_EXPERT, D_MODEL), D_FF_EXPERT ** -0.5),
    }

def reference(x_prompt, x_sample, cache_attn_k, cache_attn_v, state_hgrn, w_in, w_out,
              hg_lb_logits, hg_norm_g, norm_mix_g, norm_ffn_g, norm_final_g,
              w_route_group, w_route_expert, w_expert_gate, w_expert_up, w_expert_down):
    lb_all = jnp.cumsum(jax.nn.softmax(hg_lb_logits.astype(jnp.float32), axis=0), axis=0)
    Bp, Tp = x_prompt.shape[:2]
    Ts = x_sample.shape[1]
    pos_p = jnp.arange(Tp, dtype=jnp.int32)
    pos_s = PAST_LEN + jnp.arange(Ts, dtype=jnp.int32)
    keep_p = min(MAX_WINDOW, Tp)
    xp, xs = x_prompt, x_sample
    kp, vp, sp, ksl, vsl, ssl = [], [], [], [], [], []
    for l in range(DEPTH):
        h = rmsnorm(xp, norm_mix_g[l])
        hq, hk, hv, hlf, zg, aq, ak, av = mixer_inputs(h, w_in[l], lb_all[l], pos_p)
        s0 = jnp.zeros((Bp, HG_HEADS, HG_HEAD_DIM, HG_HEAD_DIM), jnp.float32)
        hg_o, s_fin = hgrn2_recurrence(hq, hk, hv, hlf, s0)
        res = [dilated_attention_prompt(aq, ak, av, w, d) for w, d in DILATED_PATTERNS]
        att_o = merge_dilations([r[0] for r in res], [r[1] for r in res])
        xp = xp + mixer_output(hg_o, zg, att_o, hg_norm_g[l], w_out[l], xp.dtype)
        xp = xp + channel_mixer(rmsnorm(xp, norm_ffn_g[l]), w_route_group[l], w_route_expert[l],
                                w_expert_gate[l], w_expert_up[l], w_expert_down[l])
        kp.append(ak[:, Tp - keep_p:].astype(cache_attn_k.dtype))
        vp.append(av[:, Tp - keep_p:].astype(cache_attn_v.dtype))
        sp.append(s_fin.astype(state_hgrn.dtype))
        h = rmsnorm(xs, norm_mix_g[l])
        hq, hk, hv, hlf, zg, aq, ak, av = mixer_inputs(h, w_in[l], lb_all[l], pos_s)
        hg_o, s_new = hgrn2_recurrence(hq, hk, hv, hlf, state_hgrn[l])
        k_rows = jnp.concatenate([cache_attn_k[l], ak.astype(cache_attn_k.dtype)], axis=1)
        v_rows = jnp.concatenate([cache_attn_v[l], av.astype(cache_attn_v.dtype)], axis=1)
        res = [dilated_attention_step(aq, k_rows, v_rows, w, d) for w, d in DILATED_PATTERNS]
        att_o = merge_dilations([r[0] for r in res], [r[1] for r in res])
        xs = xs + mixer_output(hg_o, zg, att_o, hg_norm_g[l], w_out[l], xs.dtype)
        xs = xs + channel_mixer(rmsnorm(xs, norm_ffn_g[l]), w_route_group[l], w_route_expert[l],
                                w_expert_gate[l], w_expert_up[l], w_expert_down[l])
        n_rows = k_rows.shape[1]
        keep_s = min(MAX_WINDOW, n_rows)
        ksl.append(k_rows[:, n_rows - keep_s:])
        vsl.append(v_rows[:, n_rows - keep_s:])
        ssl.append(s_new.astype(state_hgrn.dtype))
    y_prompt = rmsnorm(xp, norm_final_g)
    y_sample = rmsnorm(xs, norm_final_g)
    return (y_prompt, y_sample, jnp.stack(kp), jnp.stack(vp), jnp.stack(sp),
            jnp.stack(ksl), jnp.stack(vsl), jnp.stack(ssl))


_drawn_inputs = setup_inputs


def setup_inputs(seed=0):
    import zlib

    import numpy as np

    out = dict(_drawn_inputs(seed))
    spreads = {}
    factors = {'hg_norm_g': 10.937, 'norm_final_g': 8.0, 'norm_ffn_g': 3.915}
    for name, (base, spread) in spreads.items():
        noise = np.random.default_rng([zlib.crc32(name.encode()), seed]).standard_normal(out[name].shape)
        drawn = base * np.exp(spread * noise) if base else spread * noise
        out[name] = __import__('jax').numpy.asarray(drawn.astype(out[name].dtype))
    for name, factor in factors.items():
        out[name] = (out[name] * factor).astype(out[name].dtype)
    return out
```

```python
import math
from contextlib import ExitStack

import numpy as np
import concourse.bass as bass
from concourse import mybir

F32 = mybir.dt.float32
BF16 = mybir.dt.bfloat16
I32 = mybir.dt.int32
U32 = mybir.dt.uint32
ALU = mybir.AluOpType
ACT = mybir.ActivationFunctionType
AX = mybir.AxisListType

P = 128
D = 1024
KT = D // P
SEQ = 2048
TILES = SEQ // P
NS = 8
HGW, HGH, HGD = 512, 4, 128
ATW, ATH, ATD = 512, 8, 64
PAIRS = ATH // 2
HALF = 8
WIN = 2048
DILATIONS = (1, 4, 16)
IN_COLS = 4 * HGW + 3 * ATW
EPS = 1e-6
LEVELS = 7
GROUPS, PER_GROUP = 8, 8
EXPERTS = GROUPS * PER_GROUP
FF = 512
OUT_BLOCKS = 95
SLOT_BLOCKS = OUT_BLOCKS + 2
ROWS = SEQ + P

ZF, ZQ, ZV, ZK, ZA, ZW, ZG = range(7)
Z_COLUMN = {ZF: 512, ZQ: 0, ZV: 1024, ZK: 2560, ZA: 2048, ZW: 3072, ZG: 1536}


def constants():
    t = np.arange(P)
    out = {}
    out["ident"] = np.eye(P, dtype=np.float32)
    sums = np.zeros((P, LEVELS + 1, P), np.float32)
    masks = np.zeros((P, LEVELS + 1, P), np.float32)
    for l in range(LEVELS):
        h = 64 >> l
        block, right = t // (2 * h), (t % (2 * h)) >= h
        middle = block * 2 * h + h
        s = t[:, None]
        sums[:, l] = np.where(right[None], (s >= middle[None]) & (s <= t[None]), (s > t[None]) & (s < middle[None]))
        masks[:, l] = (block[:, None] == block[None]) & ~right[:, None] & right[None]
    sums[:, LEVELS] = t[:, None] <= t[None]
    masks[:, LEVELS] = np.eye(P)
    out["decay_sums"], out["pair_masks"] = sums, masks
    out["after_sum"] = (t[:, None] > t[None]).astype(np.float32)
    half = np.arange(HALF, dtype=np.float32)
    inv = (np.float32(500000.0) ** (-half / np.float32(HALF))).astype(np.float32)
    pos = np.concatenate([np.arange(SEQ), np.full(P, 4096)]).astype(np.float32)
    ang = (pos[:, None] * inv[None]).astype(np.float32)
    rot = np.stack([np.cos(ang), np.sin(ang)], 1).astype(np.float32)
    out["rotary"] = np.ascontiguousarray(rot.reshape(TILES + 1, P, 2, HALF).transpose(1, 0, 2, 3))
    return out


def bcast(ap, shape):
    return ap.broadcast_to(list(shape))


def semaphores(nc, ctx):
    made = []

    def release():
        nc.clear_and_free_semaphores(made)
        nc.all_engine_barrier()

    def sem(name):
        made.append(nc.alloc_semaphore(name=name))
        return made[-1]

    ctx.callback(release)
    return sem


def guess_rsqrt(nc, act, out, mean, log_done, at, done):
    nc.scalar.activation(out, mean, ACT.Ln).then_inc(log_done, 1)
    act.wait_ge(log_done, at)
    nc.scalar.activation(out, out, ACT.Exp, scale=-0.5).then_inc(done, 1)


def refine_rsqrt(nc, dve, out, guess, mean, tmp, steps, base, done):
    nc.vector.tensor_tensor(tmp, guess, guess, ALU.mult).then_inc(steps, 1)
    dve.wait_ge(steps, base + 1)
    nc.vector.tensor_tensor(tmp, tmp, mean, ALU.mult).then_inc(steps, 1)
    dve.wait_ge(steps, base + 2)
    nc.vector.tensor_scalar(tmp, tmp, -0.5, 1.5, ALU.mult, ALU.add).then_inc(steps, 1)
    dve.wait_ge(steps, base + 3)
    nc.vector.tensor_tensor(out, guess, tmp, ALU.mult).then_inc(done, 1)


def project_and_hgrn(nc, A, S):
    with ExitStack() as ctx:
        sb = lambda n, s, d=F32: ctx.enter_context(nc.sbuf_tensor(n, s, d))
        ps = lambda n, s: ctx.enter_context(nc.psum_tensor(n, s, F32))
        sem = semaphores(nc, ctx)

        w_in = sb("w_in", [P, KT, IN_COLS])
        ident = sb("ident1", [P, P])
        decay_sums = sb("decay_sums", [P, LEVELS + 1, P])
        pair_masks = sb("pair_masks", [P, LEVELS + 1, P], BF16)
        after_sum = sb("after_sum", [P, P])
        rotary = sb("rotary", [P, TILES + 1, 2, HALF])
        mix_gain = sb("mix_gain", [P, KT])
        head_gain = sb("head_gain", [P, HGH])
        lower = sb("lower", [P, HGW])
        one_less_lower = sb("one_less_lower", [P, HGW])
        x = sb("x", [P, D])
        xT = sb("xT", [P, 2, KT, P])
        square_sum = sb("square_sum", [P, 2])
        rstd = sb("rstd", [P, 2])
        rstd_neg = sb("rstd_neg", [P, 2])
        rstd_query = sb("rstd_query", [P, 2])
        junk = sb("junk", [P, D], BF16)
        exp_z = sb("exp_z", [P, HGW])
        sig = sb("sig", [P, HGW])
        forget = sb("forget", [P, HGW])
        logf, k_nat, v_nat, gate = (sb(n, [P, 2, HGW]) for n in ("logf", "k_nat", "v_nat", "gate"))
        q_nat = sb("q_nat", [P, HGW])
        qk = sb("qk", [P, 2, 2 * ATW])
        av = sb("av", [P, 2, ATW])
        rope_tmp = sig[:].rearrange("p (c h e) -> p c h e", c=4, e=HALF)
        qT = sb("qT", [P, HGH, P])
        kT = sb("kT", [P, HGH, P])
        attT = sb("attT", [P, 2, PAIRS, P])
        decay = sb("decay", [P, LEVELS + 1, P])
        qd = sb("qd", [P, LEVELS, P])
        q_start = sb("q_start", [P, 2, P])
        kd = sb("kd", [P, LEVELS, P])
        masked = sb("masked", [P, LEVELS + 1, P])
        attn = sb("attn", [P, 2, P])
        k_after = sb("k_after", [P, HGW])
        state = sb("state", [P, HGH, HGD])
        whole_decay = sb("whole_decay", [P, HGH])
        mean_square, rsqrt_guess, rsqrt_tmp = (sb(n, [P, 1]) for n in ("mean_square", "rsqrt_guess", "rsqrt_tmp"))
        o_mean, o_guess, o_tmp = (sb(n, [P, HGH]) for n in ("o_mean", "o_guess", "o_tmp"))
        o_sum = sb("o_sum", [P, HGH])
        o_rstd = sb("o_rstd", [P, HGH])
        hn = sb("hn", [P, HGW])
        lb_logits, lb_tmp = qk[:, 0, :].rearrange("p (r n) -> p r n", r=2), hn[:]
        hnT = sb("hnT", [P, HGH, P])

        z_ps = [ps(f"z_ps{b}", [P, 512]) for b in range(2)]
        m_ps = ps("m_ps", [P, LEVELS + 1, P])
        p_ps = ps("p_ps", [P, LEVELS + 1, P])
        t_ps = ps("t_ps", [P, HGH, P])
        o_ps = ps("o_ps", [P, HGH, HGD])

        consts_in, w_loaded, x_loaded = sem("consts_in"), [sem(f"w_loaded{g}") for g in range(7)], sem("x_loaded")
        setup_done, lower_done = sem("setup_done"), sem("lower_done")
        z_done, m_done, p_done, av_done = sem("z_done"), sem("m_done"), sem("p_done"), sem("av_done")
        xT_filled, kT_filled, qT_filled = sem("xT_filled"), sem("kT_filled"), sem("qT_filled")
        after_filled, hnT_filled, aqT_filled, akT_filled, update_filled = (
            sem(n) for n in ("after_filled", "hnT_filled", "aqT_filled", "akT_filled", "update_filled"))
        squares_done, rstd_ready, rstd_variants = sem("squares_done"), sem("rstd_ready"), sem("rstd_variants")
        exp_f_ready, exp_q_ready, exp_g_ready = sem("exp_f_ready"), sem("exp_q_ready"), sem("exp_g_ready")
        f_steps, forget_ready, logf_ready = sem("f_steps"), sem("forget_ready"), sem("logf_ready")
        forget_scaled, k_ready, rstd_steps, lower_exp, q_start_ready = (
            sem(n) for n in ("forget_scaled", "k_ready", "rstd_steps", "lower_exp", "q_start_ready"))
        q_steps, q_ready, g_steps, gate_ready = sem("q_steps"), sem("q_ready"), sem("g_steps"), sem("gate_ready")
        v_ready, ak_copied, aq_copied, av_ready = (sem(n) for n in ("v_ready", "ak_copied", "aq_copied", "av_ready"))
        rope_products, rotated = sem("rope_products"), sem("rotated")
        xT_ready, kT_ready, qT_ready, hnT_ready, aqT_ready, akT_ready = (
            sem(n) for n in ("xT_ready", "kT_ready", "qT_ready", "hnT_ready", "aqT_ready", "akT_ready"))
        decay_ready, qd_ready, kd_ready, masked_ready, attn_ready = (
            sem(n) for n in ("decay_ready", "qd_ready", "kd_ready", "masked_ready", "attn_ready"))
        after_ready, k_after_ready, state_ready, whole_ready = (
            sem(n) for n in ("after_ready", "k_after_ready", "state_ready", "whole_ready"))
        cache_stored = sem("cache_stored")
        o_squares, o_rstd_steps, hn_scaled, hn_ready = (
            sem(n) for n in ("o_squares", "o_rstd_steps", "hn_scaled", "hn_ready"))
        qk_stored, av_stored, aqT_stored, akT_stored, hnT_stored, state_stored = (
            sem(n) for n in ("qk_stored", "av_stored", "aqT_stored", "akT_stored", "hnT_stored", "state_stored"))

        mean_ready, log_ready, guess_ready, o_mean_ready, o_log_ready, o_guess_ready, o_rstd_ready = (
            sem(n) for n in ("mean_ready", "log_ready", "guess_ready", "o_mean_ready", "o_log_ready", "o_guess_ready",
                             "o_rstd_ready"))

        def turns(eng, body):
            body(0, 0, past=0, more=True)
            body(1, 1, past=1, more=True)
            with eng.Fori(0, (TILES - 2) // 2) as i:
                for u in range(2):
                    body(2 * i + 2 + u, u, past=2, more=True)
            body(TILES, 0, past=2, more=False)

        block = ctx.enter_context(nc.Block())


        @block.sync
        def _(sp):
            for dst, src in ((ident, A["ident"]), (mix_gain, A["mix_gain"])):
                sp.dma_start(dst[:], src).then_inc(consts_in, 16)
            w_view = A["w_in"][0].rearrange("(t p) n -> p t n", p=P)

            def load_w(g):
                c = Z_COLUMN[g]
                sp.dma_start(w_in[:, :, c:c + 512], w_view[:, :, c:c + 512]).then_inc(w_loaded[g], 16)

            def load_rest():
                for dst, src in ((rotary, A["rotary"]), (decay_sums, A["decay_sums"]), (masked, A["pair_masks"]),
                                 (after_sum, A["after_sum"]),
                                 (head_gain, A["head_gain"])):
                    sp.dma_start(dst[:], src).then_inc(consts_in, 16)
                for r in range(2):
                    sp.dma_start(lb_logits[:, r, :], bcast(A["hg_lb_logits"][r:r + 1, :], (P, HGW)))\
                      .then_inc(consts_in, 16)

            def store_hgrn(j):
                sp.wait_ge(hnT_ready, j + 1)
                sp.dma_start(S["catT"][0:HGH, :, bass.ds(j * P, P)].rearrange("h p t -> p h t"), hnT[:])\
                  .then_inc(hnT_stored, 16)

            def store_tile(j, v):
                sp.wait_ge(av_ready, j + 1)
                sp.dma_start(A["new_v_prompt"][bass.ds(j * P, P), :], av[:, v, :]).then_inc(av_stored, 16)
                sp.wait_ge(rotated, 2 * j + 2)
                sp.wait_ge(aqT_ready, j + 1)
                sp.dma_start(A["new_k_prompt"][bass.ds(j * P, P), :], qk[:, v, ATW:]).then_inc(qk_stored, 16)
                sp.dma_start(S["attqT"][:, :, bass.ds(j * P, P)].rearrange("c p t -> p c t"), attT[:, 0])\
                  .then_inc(aqT_stored, 16)
                sp.wait_ge(akT_ready, j + 1)
                sp.dma_start(S["attkT"][:, :, bass.ds(j * P, P)].rearrange("c p t -> p c t"), attT[:, 1])\
                  .then_inc(akT_stored, 16)

            def body(n, u, past, more):
                if past:
                    sp.wait_ge(xT_filled, 2 * n)
                    sp.wait_ge(squares_done, n)
                if more:
                    sp.dma_start(x[:], A["x_prompt"][0, bass.ds(n * P, P), :]).then_inc(x_loaded, 16)
                else:
                    sp.dma_start(x[0:NS, :], A["x_sample"][:, 0, :]).then_inc(x_loaded, 16)
                if past == 0:
                    load_w(0)
                    load_rest()
                    load_w(1)
                if past == 1:
                    for g in range(2, 7):
                        load_w(g)
                if past:
                    for name in ("k", "v"):
                        src = A["cache_attn_" + name][0].rearrange("b w h e -> b w (h e)")
                        rows = bass.ds(n * P - P + 1, P if more else P - 1)
                        to = bass.ds(n * P - P, P if more else P - 1)
                        sp.dma_start(A[f"new_{name}_sample"][:, to, :], src[:, rows, :]).then_inc(cache_stored, 16)
                if past == 2:
                    store_tile(n - 2, u)
                    store_hgrn(n - 2)

            turns(sp, body)
            store_tile(TILES - 1, 1)
            store_hgrn(TILES - 1)
            sp.wait_ge(state_ready, HGH * TILES)
            sp.dma_start(A["new_hgrn_prompt"].rearrange("h k v -> k h v"), state[:]).then_inc(state_stored, 16)
            sp.wait_ge(gate_ready, TILES + 1)
            sp.wait_ge(av_ready, TILES + 1)
            sp.wait_ge(v_ready, TILES + 1)
            sp.wait_ge(rotated, 2 * TILES + 2)
            for c, src in enumerate((q_nat[0:NS, :], k_nat[0:NS, 0], forget[0:NS, :], v_nat[0:NS, 0], gate[0:NS, 0],
                                     qk[0:NS, 0, 0:ATW], qk[0:NS, 0, ATW:], av[0:NS, 0])):
                sp.dma_start(S["sample"][:, c * 512:(c + 1) * 512], src).then_inc(state_stored, 16)
            sp.wait_ge(state_stored, 16 * 9)
            sp.wait_ge(cache_stored, 32 * TILES)
            sp.wait_ge(av_stored, 16 * TILES)
            sp.wait_ge(qk_stored, 16 * TILES)
            sp.wait_ge(aqT_stored, 16 * TILES)
            sp.wait_ge(akT_stored, 16 * TILES)
            sp.wait_ge(hnT_stored, 16 * TILES + 16)

        @block.tensor
        def _(pe):
            z_bank_read = [exp_f_ready, q_ready, v_ready, ak_copied, aq_copied, av_ready, gate_ready]

            def transposes(srcs, filled):
                for c, src in enumerate(srcs):
                    last = nc.tensor.transpose(t_ps[:, c, :], src, ident[:])
                last.then_inc(filled, 1)

            def transpose_x(half):
                transposes([x[:, (4 * half + c) * P:(4 * half + c + 1) * P] for c in range(4)], xT_filled)

            def product(j, h):
                pe.wait_ge(qd_ready, HGH * j + h + 1)
                pe.wait_ge(kd_ready, HGH * j + h + 1)
                if not (isinstance(j, int) and HGH * j + h < 1):
                    pe.wait_ge(masked_ready, HGH * j + h)
                for l in range(LEVELS):
                    nc.tensor.matmul(p_ps[:, l, :], kd[:, l, :], qd[:, l, :], start=True, stop=True)
                nc.tensor.matmul(p_ps[:, LEVELS, :], kT[:, h, :], qT[:, h, :], start=True, stop=True).then_inc(p_done, 1)

            def sums(j, v, h):
                if not (isinstance(j, int) and HGH * j + h < 1):
                    pe.wait_ge(decay_ready, HGH * j + h)
                if h == 0:
                    pe.wait_ge(logf_ready, j + 1)
                for b in range(2):
                    last = nc.tensor.matmul(m_ps[:, 4 * b:4 * b + 4, :], logf[:, v, h * HGD:(h + 1) * HGD],
                                            decay_sums[:, 4 * b:4 * b + 4, :], start=True, stop=True)
                last.then_inc(m_done, 1)

            def output(j, v, h):
                pe.wait_ge(attn_ready, HGH * j + h + 1)
                pe.wait_ge(q_start_ready, HGH * j + h + 1)
                if h == 0 and not (isinstance(j, int) and j < 1):
                    pe.wait_ge(hn_scaled, j)
                nc.tensor.matmul(o_ps[:, h, :], attn[:, h % 2, :], v_nat[:, v, h * HGD:(h + 1) * HGD],
                                 start=True, stop=False)
                nc.tensor.matmul(o_ps[:, h, :], q_start[:, h % 2, :], state[:, h, :],
                                 start=False, stop=True).then_inc(av_done, 1)

            def body(n, u, past, more):
                j, v = n - 1, 1 - u
                for g in range(7):
                    if g == 0:
                        pe.wait_ge(xT_ready, 2 * n + 2)
                    if past == 0:
                        pe.wait_ge(w_loaded[g], 16)
                    if g >= 2:
                        pe.wait_ge(z_bank_read[g - 2], n + 1)
                    elif past:
                        pe.wait_ge(z_bank_read[g + 5], n)
                    for t in range(KT):
                        last = nc.tensor.matmul(z_ps[(u + g) % 2][:], xT[:, u, t, :],
                                                w_in[:, t, Z_COLUMN[g]:Z_COLUMN[g] + 512],
                                                start=(t == 0), stop=(t == KT - 1))
                    last.then_inc(z_done, 1)
                    if past and g == 0:
                        if past == 2:
                            pe.wait_ge(state_ready, HGH * j)
                        pe.wait_ge(k_ready, j + 1)
                        transposes([k_nat[:, v, h * P:(h + 1) * P] for h in range(HGH)], kT_filled)
                        pe.wait_ge(kT_ready, j + 1)
                        pe.wait_ge(q_ready, j + 1)
                        transposes([q_nat[:, h * P:(h + 1) * P] for h in range(HGH)], qT_filled)
                    if past and g == 1:
                        if past == 1:
                            pe.wait_ge(consts_in, 16 * 9)
                        sums(j, v, 0)
                        pe.wait_ge(qT_ready, j + 1)
                        nc.tensor.matmul(t_ps[:], after_sum[:], logf[:, v, :], start=True, stop=True)\
                          .then_inc(after_filled, 1)
                        if past == 2:
                            pe.wait_ge(after_ready, j + 1)
                            pe.wait_ge(hn_ready, n - 1)
                            transposes([hn[:, h * P:(h + 1) * P] for h in range(HGH)], hnT_filled)
                    if past and g == 2:
                        product(j, 0)
                        sums(j, v, 1)
                        if past == 2:
                            pe.wait_ge(hnT_ready, n - 1)
                        else:
                            pe.wait_ge(after_ready, j + 1)
                        pe.wait_ge(rotated, 2 * j + 2)
                        transposes([qk[:, v, c * P:(c + 1) * P] for c in range(PAIRS)], aqT_filled)
                    if past and g == 3:
                        output(j, v, 0)
                        product(j, 1)
                        sums(j, v, 2)
                        pe.wait_ge(aqT_ready, j + 1)
                        transposes([qk[:, v, ATW + c * P:ATW + (c + 1) * P] for c in range(PAIRS)], akT_filled)
                    if g == 4:
                        if past:
                            output(j, v, 1)
                            product(j, 2)
                            sums(j, v, 3)
                        if more:
                            if past:
                                pe.wait_ge(akT_ready, j + 1)
                            pe.wait_ge(x_loaded, 16 * n + 32)
                            transpose_x(0)
                    if g == 5:
                        if past:
                            output(j, v, 2)
                            product(j, 3)
                        if more:
                            pe.wait_ge(xT_ready, 2 * n + 3)
                            transpose_x(1)
                    if past and g == 6:
                        output(j, v, 3)
                        if more:
                            pe.wait_ge(xT_ready, 2 * n + 4)
                        else:
                            pe.wait_ge(akT_ready, j + 1)
                        pe.wait_ge(k_after_ready, j + 1)
                        for h in range(HGH):
                            last = nc.tensor.matmul(t_ps[:, h, :], k_after[:, h * HGD:(h + 1) * HGD],
                                                    v_nat[:, v, h * HGD:(h + 1) * HGD], start=True, stop=True)
                        last.then_inc(update_filled, 1)

            pe.wait_ge(consts_in, 32)
            pe.wait_ge(x_loaded, 16)
            transpose_x(0)
            pe.wait_ge(xT_ready, 1)
            transpose_x(1)
            turns(pe, body)
            pe.wait_ge(state_ready, HGH * TILES)
            pe.wait_ge(hn_ready, TILES)
            transposes([hn[:, h * P:(h + 1) * P] for h in range(HGH)], hnT_filled)

        @block.scalar
        def _(act):
            def decays(j, h):
                act.wait_ge(m_done, HGH * j + h + 1)
                if not (isinstance(j, int) and HGH * j + h < 1):
                    act.wait_ge(kd_ready, HGH * j + h)
                    act.wait_ge(whole_ready, HGH * j + h)
                nc.scalar.activation(decay[:], m_ps[:], ACT.Exp).then_inc(decay_ready, 1)

            def squares(n, u):
                act.wait_ge(x_loaded, 16 * n + 16)
                nc.scalar.activation(junk[:], x[:], ACT.Square, accum_out=square_sum[:, u:u + 1])\
                  .then_inc(squares_done, 1)

            def guess(n):
                act.wait_ge(mean_ready, n + 1)
                guess_rsqrt(nc, act, rsqrt_guess[:], mean_square[:], log_ready, n + 1, guess_ready)

            def body(n, u, past, more):
                j = n - 1
                bank = lambda g: z_ps[(u + g) % 2][:]
                act.wait_ge(rstd_variants, 2 * n + 2)
                act.wait_ge(z_done, 7 * n + 1)
                if past:
                    act.wait_ge(gate_ready, n)
                nc.scalar.activation(exp_z[:], bank(ZF), ACT.Exp, scale=rstd_neg[:, u:u + 1]).then_inc(exp_f_ready, 1)
                act.wait_ge(z_done, 7 * n + 2)
                act.wait_ge(f_steps, 2 * n + 1)
                nc.scalar.activation(exp_z[:], bank(ZQ), ACT.Exp, scale=rstd_neg[:, u:u + 1]).then_inc(exp_q_ready, 1)
                if past:
                    decays(j, 0)
                    act.wait_ge(after_filled, j + 1)
                    if past == 2:
                        act.wait_ge(update_filled, j)
                    nc.scalar.activation(k_after[:], t_ps[:], ACT.Exp).then_inc(after_ready, 1)
                act.wait_ge(forget_ready, n + 1)
                nc.scalar.activation(logf[:, u, :], forget[:], ACT.Ln).then_inc(logf_ready, 1)
                act.wait_ge(z_done, 7 * n + 3)
                nc.scalar.activation(v_nat[:, u, :], bank(ZV), ACT.Copy, scale=rstd[:, u:u + 1]).then_inc(v_ready, 1)
                if past:
                    decays(j, 1)
                act.wait_ge(z_done, 7 * n + 4)
                if past == 2:
                    act.wait_ge(qk_stored, 16 * n - 16)
                nc.scalar.activation(qk[:, u, ATW:], bank(ZK), ACT.Copy, scale=rstd[:, u:u + 1]).then_inc(ak_copied, 1)
                if past:
                    decays(j, 2)
                act.wait_ge(z_done, 7 * n + 5)
                nc.scalar.activation(qk[:, u, 0:ATW], bank(ZA), ACT.Copy, scale=rstd_query[:, u:u + 1])\
                  .then_inc(aq_copied, 1)
                if past:
                    decays(j, 3)
                act.wait_ge(z_done, 7 * n + 6)
                if past == 2:
                    act.wait_ge(av_stored, 16 * n - 16)
                nc.scalar.activation(av[:, u, :], bank(ZW), ACT.Copy, scale=rstd[:, u:u + 1]).then_inc(av_ready, 1)
                if more:
                    if past:
                        act.wait_ge(rstd_ready, n + 1)
                    if past == 2:
                        act.wait_ge(o_squares, HGH * (n - 1))
                    squares(n + 1, 1 - u)
                act.wait_ge(z_done, 7 * n + 7)
                act.wait_ge(q_steps, 2 * n + 1)
                nc.scalar.activation(exp_z[:], bank(ZG), ACT.Exp, scale=rstd_neg[:, u:u + 1]).then_inc(exp_g_ready, 1)
                if past:
                    act.wait_ge(av_done, HGH * n)
                    act.wait_ge(squares_done, n + 1 + more)
                    for h in range(HGH):
                        nc.scalar.activation(junk[:, h * HGD:(h + 1) * HGD], o_ps[:, h, :], ACT.Square,
                                             accum_out=o_sum[:, h:h + 1]).then_inc(o_squares, 1)
                if more:
                    guess(n + 1)
                if past:
                    act.wait_ge(o_mean_ready, j + 1)
                    guess_rsqrt(nc, act, o_guess[:], o_mean[:], o_log_ready, j + 1, o_guess_ready)

            squares(0, 0)
            guess(0)
            act.wait_ge(lower_done, 3)
            nc.scalar.activation(lb_logits[:], lb_logits[:], ACT.Exp).then_inc(lower_exp, 1)
            turns(act, body)

        @block.gpsimd
        def _(pool):
            def keys(j, h):
                pool.wait_ge(kT_ready, j + 1)
                pool.wait_ge(decay_ready, HGH * j + h + 1)
                if not (isinstance(j, int) and HGH * j + h < 1):
                    pool.wait_ge(p_done, HGH * j + h)
                nc.gpsimd.tensor_tensor(kd[:], decay[:, 0:LEVELS, :],
                                        bcast(kT[:, h:h + 1, :], (P, LEVELS, P)), ALU.mult).then_inc(kd_ready, 1)

            def body(n, u, past, more):
                j, v = n - 1, 1 - u
                if not past:
                    return
                keys(j, 0)
                pool.wait_ge(after_ready, j + 1)
                nc.gpsimd.tensor_tensor(k_after[:], k_after[:], k_nat[:, v, :], ALU.mult).then_inc(k_after_ready, 1)
                for h in range(1, HGH):
                    keys(j, h)

            turns(pool, body)

        @block.vector
        def _(dve):
            def lower_bound():
                dve.wait_ge(consts_in, 16 * 9)
                a, b = lb_logits[:, 0, :], lb_logits[:, 1, :]
                nc.vector.tensor_tensor(lb_tmp[:], a, b, ALU.max).then_inc(lower_done, 1)
                dve.wait_ge(lower_done, 1)
                nc.vector.tensor_tensor(a, a, lb_tmp[:], ALU.subtract).then_inc(lower_done, 1)
                nc.vector.tensor_tensor(b, b, lb_tmp[:], ALU.subtract).then_inc(lower_done, 1)

            def lower_bound_end():
                dve.wait_ge(lower_exp, 1)
                a, b = lb_logits[:, 0, :], lb_logits[:, 1, :]
                nc.vector.tensor_tensor(lb_tmp[:], a, b, ALU.add).then_inc(lower_done, 1)
                dve.wait_ge(lower_done, 4)
                nc.vector.reciprocal(lb_tmp[:], lb_tmp[:]).then_inc(lower_done, 1)
                dve.wait_ge(lower_done, 5)
                nc.vector.tensor_tensor(lower[:], a, lb_tmp[:], ALU.mult).then_inc(lower_done, 1)
                dve.wait_ge(lower_done, 6)
                nc.vector.tensor_scalar(one_less_lower[:], lower[:], -1.0, 1.0, ALU.mult, ALU.add)\
                  .then_inc(lower_done, 1)
                dve.wait_ge(lower_done, 7)

            def drain_x(n, u, half):
                dve.wait_ge(xT_filled, 2 * n + half + 1)
                nc.vector.tensor_tensor(xT[:, u, 4 * half:4 * half + 4, :], t_ps[:],
                                        bcast(mix_gain[:, 4 * half:4 * half + 4].unsqueeze(2), (P, 4, P)), ALU.mult)\
                  .then_inc(xT_ready, 1)

            def norm(n, u):
                dve.wait_ge(squares_done, n + 1)
                c = slice(u, u + 1)
                nc.vector.tensor_scalar(mean_square[:], square_sum[:, c], 1.0 / D, EPS, ALU.mult, ALU.add)\
                  .then_inc(mean_ready, 1)

            def norm_end(n, u):
                c = slice(u, u + 1)
                dve.wait_ge(guess_ready, n + 1)
                refine_rsqrt(nc, dve, rstd[:, c], rsqrt_guess[:], mean_square[:], rsqrt_tmp[:], rstd_steps, 3 * n, rstd_ready)
                dve.wait_ge(rstd_ready, n + 1)
                nc.vector.tensor_scalar(rstd_neg[:, c], rstd[:, c], -1.0, None, ALU.mult).then_inc(rstd_variants, 1)
                nc.vector.tensor_scalar(rstd_query[:, c], rstd[:, c], ATD ** -0.5, None, ALU.mult)\
                  .then_inc(rstd_variants, 1)

            def sigmoid(src, src_ready, steps, n):
                dve.wait_ge(src_ready, n + 1)
                nc.vector.tensor_scalar(sig[:], src[:], 1.0, None, ALU.add).then_inc(steps, 1)
                dve.wait_ge(steps, 2 * n + 1)
                nc.vector.reciprocal(sig[:], sig[:]).then_inc(steps, 1)
                dve.wait_ge(steps, 2 * n + 2)

            def queries(j, h):
                dve.wait_ge(decay_ready, HGH * j + h + 1)
                if not (isinstance(j, int) and HGH * j + h < 1):
                    dve.wait_ge(p_done, HGH * j + h)
                nc.vector.tensor_tensor(qd[:], decay[:, 0:LEVELS, :],
                                        bcast(qT[:, h:h + 1, :], (P, LEVELS, P)), ALU.mult).then_inc(qd_ready, 1)
                if not (isinstance(j, int) and HGH * j + h < 2):
                    dve.wait_ge(av_done, HGH * j + h - 1)
                nc.vector.tensor_tensor(q_start[:, h % 2, :], decay[:, LEVELS, :], qT[:, h, :], ALU.mult)\
                  .then_inc(q_start_ready, 1)
                nc.vector.tensor_copy(whole_decay[:, h:h + 1], decay[:, LEVELS, P - 1:P]).then_inc(whole_ready, 1)

            def scores(j, h):
                dve.wait_ge(p_done, HGH * j + h + 1)
                nc.vector.tensor_tensor(masked[:], p_ps[:], pair_masks[:], ALU.mult).then_inc(masked_ready, 1)
                dve.wait_ge(masked_ready, HGH * j + h + 1)
                if not (isinstance(j, int) and HGH * j + h < 2):
                    dve.wait_ge(av_done, HGH * j + h - 1)
                nc.vector.reduce_sum(attn[:, h % 2, :], masked[:].rearrange("p l t -> p t l"), axis=AX.X)\
                  .then_inc(attn_ready, 1)

            def rope(n, u):
                dve.wait_ge(ak_copied, n + 1)
                dve.wait_ge(aq_copied, n + 1)
                heads = qk[:, u, :].rearrange("p (h e) -> p h e", e=ATD)
                x1, x2 = heads[:, :, 0:HALF], heads[:, :, HALF:2 * HALF]
                cos = bcast(rotary[:, bass.ds(n, 1), 0, :], (P, 2 * ATH, HALF))
                sin = bcast(rotary[:, bass.ds(n, 1), 1, :], (P, 2 * ATH, HALF))
                for c, (a, b) in enumerate(((x1, cos), (x2, sin), (x2, cos), (x1, sin))):
                    nc.vector.tensor_tensor(rope_tmp[:, c], a, b, ALU.mult).then_inc(rope_products, 1)
                dve.wait_ge(rope_products, 4 * n + 4)
                nc.vector.tensor_tensor(x1, rope_tmp[:, 0], rope_tmp[:, 1], ALU.subtract).then_inc(rotated, 1)
                nc.vector.tensor_tensor(x2, rope_tmp[:, 2], rope_tmp[:, 3], ALU.add).then_inc(rotated, 1)

            def hn_drain(j):
                dve.wait_ge(hnT_filled, j + 1)
                dve.wait_ge(hnT_stored, 16 * j + 16)
                nc.vector.tensor_tensor(hnT[:], t_ps[:], bcast(head_gain[:].unsqueeze(2), (P, HGH, P)), ALU.mult)\
                  .then_inc(hnT_ready, 1)

            def body(n, u, past, more):
                j, v = n - 1, 1 - u
                bank = lambda g: z_ps[(u + g) % 2][:]
                if past:
                    dve.wait_ge(kT_filled, j + 1)
                    nc.vector.tensor_copy(kT[:], t_ps[:]).then_inc(kT_ready, 1)
                    dve.wait_ge(qT_filled, j + 1)
                    nc.vector.tensor_copy(qT[:], t_ps[:]).then_inc(qT_ready, 1)
                    dve.wait_ge(qT_ready, j + 1)
                sigmoid(exp_z, exp_f_ready, f_steps, n)
                if past:
                    dve.wait_ge(logf_ready, n)
                nc.vector.tensor_tensor(forget[:], sig[:], one_less_lower[:], ALU.mult).then_inc(forget_scaled, 1)
                dve.wait_ge(forget_scaled, n + 1)
                nc.vector.tensor_tensor(forget[:], forget[:], lower[:], ALU.add).then_inc(forget_ready, 1)
                dve.wait_ge(forget_ready, n + 1)
                if past == 2:
                    dve.wait_ge(k_after_ready, n - 1)
                nc.vector.tensor_scalar(k_nat[:, u, :], forget[:], -1.0, 1.0, ALU.mult, ALU.add).then_inc(k_ready, 1)
                sigmoid(exp_z, exp_q_ready, q_steps, n)
                nc.vector.scalar_tensor_tensor(q_nat[:], bank(ZQ), rstd[:, u:u + 1], sig[:], ALU.mult, ALU.mult)\
                  .then_inc(q_ready, 1)
                if past:
                    queries(j, 0)
                    if past == 2:
                        hn_drain(n - 2)
                    scores(j, 0)
                    queries(j, 1)
                    dve.wait_ge(aqT_filled, j + 1)
                    if past == 2:
                        dve.wait_ge(aqT_stored, 16 * j)
                    nc.vector.tensor_copy(attT[:, 0], t_ps[:]).then_inc(aqT_ready, 1)
                    scores(j, 1)
                    queries(j, 2)
                    dve.wait_ge(akT_filled, j + 1)
                    if past == 2:
                        dve.wait_ge(akT_stored, 16 * j)
                    nc.vector.tensor_copy(attT[:, 1], t_ps[:]).then_inc(akT_ready, 1)
                    scores(j, 2)
                    queries(j, 3)
                if more:
                    drain_x(n + 1, v, 0)
                rope(n, u)
                if past:
                    scores(j, 3)
                if more:
                    drain_x(n + 1, v, 1)
                    norm(n + 1, v)
                dve.wait_ge(rotated, 2 * n + 2)
                sigmoid(exp_z, exp_g_ready, g_steps, n)
                nc.vector.scalar_tensor_tensor(gate[:, u, :], bank(ZG), rstd[:, u:u + 1], sig[:], ALU.mult, ALU.mult)\
                  .then_inc(gate_ready, 1)
                if more:
                    norm_end(n + 1, v)
                if past:
                    dve.wait_ge(update_filled, j + 1)
                    dve.wait_ge(whole_ready, HGH * j + HGH)
                    for h in range(HGH):
                        nc.vector.scalar_tensor_tensor(state[:, h, :], state[:, h, :], whole_decay[:, h:h + 1],
                                                       t_ps[:, h, :], ALU.mult, ALU.add).then_inc(state_ready, 1)
                    dve.wait_ge(o_squares, HGH * j + HGH)
                    nc.vector.tensor_scalar(o_mean[:], o_sum[:], 1.0 / HGD, EPS, ALU.mult, ALU.add)\
                      .then_inc(o_mean_ready, 1)
                    dve.wait_ge(o_guess_ready, j + 1)
                    refine_rsqrt(nc, dve, o_rstd[:], o_guess[:], o_mean[:], o_tmp[:], o_rstd_steps, 3 * j, o_rstd_ready)
                    dve.wait_ge(o_rstd_ready, j + 1)
                    nc.vector.tensor_tensor(hn[:].rearrange("p (h e) -> p h e", h=HGH), o_ps[:],
                                            bcast(o_rstd[:].unsqueeze(2), (P, HGH, HGD)), ALU.mult)\
                      .then_inc(hn_scaled, 1)
                    dve.wait_ge(hn_scaled, j + 1)
                    nc.vector.tensor_tensor(hn[:], hn[:], gate[:, v, :], ALU.mult).then_inc(hn_ready, 1)

            nc.vector.memset(state[:], 0.0).then_inc(setup_done, 1)
            nc.vector.memset(hnT[:], 0.0).then_inc(hnT_stored, 16)
            dve.wait_ge(consts_in, 32)
            drain_x(0, 0, 0)
            drain_x(0, 0, 1)
            norm(0, 0)
            norm_end(0, 0)
            dve.wait_ge(consts_in, 16 * 9)
            nc.vector.tensor_copy(pair_masks[:], masked[:]).then_inc(setup_done, 1)
            dve.wait_ge(setup_done, 2)
            lower_bound()
            lower_bound_end()
            turns(dve, body)
            hn_drain(TILES - 1)


NEG = -1e30


def tile_start(d, m):
    return d * P * (m // d) + m % d


def query_units():
    units = []
    for p, d in enumerate(DILATIONS):
        alone = [(p, m, m, P) for m in range(min(d, TILES))]
        paired = [(p, m, m - d, 2 * P) for m in range(d, TILES)]
        if d == 1:
            units.append(alone + paired[:1])
            paired = paired[1:]
        else:
            units += [alone[k:k + 4] for k in range(0, len(alone), 4)]
        units += [paired[k:k + 2] for k in range(0, len(paired), 2)]
    return units


def key_units():
    units = []
    for p, d in enumerate(DILATIONS):
        both = [(p, m, m, 2 * P) for m in range(TILES - d)]
        last = [(p, m, m, P) for m in range(max(TILES - d, 0), TILES)]
        if d == 1:
            units += [both[k:k + 2] for k in range(0, len(both) - 1, 2)] + [both[-1:] + last]
        else:
            units += [both[k:k + 2] for k in range(0, len(both), 2)] + [last[k:k + 4] for k in range(0, len(last), 4)]
    return units


def attention_constants():
    t = np.arange(P)
    own = np.where(t[None] <= t[:, None], 0.0, NEG).astype(np.float32)
    prev = np.where(t[None] >= t[:, None], 0.0, NEG).astype(np.float32)
    return {"band_masks": np.concatenate([prev, own, prev, own, own, own, own, own,
                                          own.T, prev.T, own.T, prev.T, own.T, own.T, own.T, own.T], axis=1)}


def prompt_attention(nc, A, S):
    QU, KU = query_units(), key_units()
    V_LOADS = 12
    NA, NB = len(QU) + 1, len(KU)
    with ExitStack() as ctx:
        sb = lambda n, s, d=F32: ctx.enter_context(nc.sbuf_tensor(n, s, d))
        ps = lambda n, s: ctx.enter_context(nc.psum_tensor(n, s, F32))
        sem = semaphores(nc, ctx)
        qT = sb("aqT", [P, 2, SEQ])
        kT = sb("akT", [P, 2, 2, SEQ])
        v1 = sb("v1", [P, 2, 3, TILES, 3 * ATD])
        ident = sb("ident2", [P, P])
        ident_bf = sb("ident_bf", [P, P], BF16)
        blank = sb("blank", [P, D])
        blanked, cleared = sem("blanked"), sem("cleared")
        masks = sb("masks", [P, 4, 512], BF16)
        staged = sb("staged", [P, 4, 512])
        zeros = sb("zeros", [1, P], BF16)
        take_peak = sb("take_peak", [P, 2, P], BF16)
        peak = sb("peak", [P, 2, P])
        peakT = sb("peakT", [3 * TILES, 2, P])
        peak_rows = sb("peak_rows", [33, 3, SEQ])
        peaks = sb("peaks", [P, 2, SEQ], BF16)
        probs = sb("probs", [P, 2, 512])
        denominator = sb("denominator", [P, SEQ])
        att = sb("att", [P, SEQ])
        a_ps = [ps(f"a_ps{b}", [P, 512]) for b in range(2)]
        b_ps = [ps(f"b_ps{b}", [P, 512]) for b in range(2)]
        out_ps = ps("out_ps", [P, SEQ])

        consts_in, constants_ready, ones_ready = sem("consts_in2"), sem("constants_ready2"), sem("ones_ready2")
        qk_loaded, v_loaded = [sem(f"qk_loaded{u}") for u in range(2)], [sem(f"v_loaded{u}") for u in range(2)]
        query_scores, peaks_read = sem("query_scores"), sem("peaks_read")
        rows_loaded = [sem(f"rows_loaded{a}") for a in range(2)]
        rows_max, peak_hi_ready, peak_lo_ready = (sem(n) for n in ("rows_max", "peak_hi_ready", "peak_lo_ready"))
        key_scores, probs_ready, probs_used, head_done = (
            sem(n) for n in ("key_scores", "probs_ready", "probs_used", "head_done"))
        acc_copied, den_ready, att_ready, att_stored = (sem(n) for n in ("acc_copied", "den_ready", "att_ready", "att_stored"))

        def tokens(ap, d, m, n):
            s = tile_start(d, m)
            return ap[:, s:s + d * (n - 1) + 1:d]

        def later_pairs(eng, body):
            with eng.Fori(0, (PAIRS - 2) // 2) as i:
                body(2 * i + 1, 1, i)
                body(2 * i + 2, 0, i + 1)
            body(PAIRS - 1, 1, (PAIRS - 1) // 2)

        block = ctx.enter_context(nc.Block())

        @block.sync
        def _(sp):
            sp.dma_start(ident[:], A["ident"]).then_inc(consts_in, 16)
            sp.dma_start(staged[:], A["band_masks"].rearrange("p (k n) -> p k n", k=4)).then_inc(consts_in, 16)

            def load(c, u):
                sp.wait_ge(head_done, 2 * c + 2)
                sp.dma_start(qT[:, u, :], S["attqT"][bass.ds(c, 1), :, :].rearrange("a p t -> p (a t)"))\
                  .then_inc(qk_loaded[u], 16)
                for a in range(2):
                    h = slice(a * ATD, (a + 1) * ATD)
                    sp.dma_start(kT[h, u, a, :], S["attkT"][bass.ds(c, 1), h, :].rearrange("a p t -> p (a t)"))\
                      .then_inc(qk_loaded[u], 16)
                for a in range(2):
                    cols = bass.ds(c * P + a * ATD, ATD)
                    v = A["new_v_prompt"][:, cols]
                    dst = lambda p: v1[:, u, p, :, 2 * a * ATD:(2 * a + 1) * ATD]
                    sp.dma_start(dst(0), v.rearrange("(m i) e -> i m e", i=P)).then_inc(v_loaded[u], 16)
                    for b in range(4):
                        sp.dma_start(dst(1)[:, 4 * b:4 * b + 4], A["new_v_prompt"][512 * b:512 * b + 512, cols]
                                     .rearrange("(i r) e -> i r e", r=4)).then_inc(v_loaded[u], 16)
                    sp.dma_start(dst(2), v.rearrange("(i m) e -> i m e", m=TILES)).then_inc(v_loaded[u], 16)

            def store(c):
                sp.wait_ge(att_ready, 8 * c + 12)
                sp.dma_start(S["catT"][bass.ds(c + HGH, 1), :, :].rearrange("a p t -> p (a t)"), att[:])\
                  .then_inc(att_stored, 16)

            load(0, 0)
            load(1, 1)
            with sp.Fori(0, (PAIRS - 2) // 2) as i:
                for u in range(2):
                    load(2 * i + u + 2, u)
                    store(2 * i + u)
            store(PAIRS - 2)
            store(PAIRS - 1)
            sp.wait_ge(att_stored, 16 * PAIRS + 16)

        @block.gpsimd
        def _(pool):
            made = [(v1[:, :, :, :, ATD:2 * ATD], 1.0), (kT[ATD:P, :, 0, :], 0.0), (kT[0:ATD, :, 1, :], 0.0),
                    (take_peak[:], 0.0)]
            made += [(take_peak[row:row + 1, row // 32 % 2, :], 1.0) for row in (0, 32, 64, 96)]
            for n, (dst, value) in enumerate(made):
                if n:
                    pool.wait_ge(ones_ready, n)
                nc.gpsimd.memset(dst, value).then_inc(ones_ready, 1)
            pool.wait_ge(ones_ready, len(made))
            nc.gpsimd.memset(blank[:], 0.0).then_inc(blanked, 1)
            pool.wait_ge(blanked, 1)
            for c in range(1, PAIRS):
                first, end = (c - 1) * OUT_BLOCKS // 3, c * OUT_BLOCKS // 3
                pool.wait_ge(v_loaded[c % 2], 16 * V_LOADS * (c // 2 + 1))
                pool.dma_start(S["y_slots"][first * P:end * P, :].rearrange("(b p) d -> p b d", p=P),
                               blank[:].unsqueeze(1).broadcast_to([P, end - first, D])).then_inc(cleared, 16)
            pool.wait_ge(cleared, 16 * (PAIRS - 1))

        @block.scalar
        def _(act):
            def rows(c, a):
                act.wait_ge(peaks_read, 2 * c * NA + (a + 1) * NA + 2)
                act.dma_start(peak_rows[32 * a:32 * a + 1, :, :].rearrange("o p (m i) -> o (p m) i", i=P),
                              peakT[:, a, :]).then_inc(rows_loaded[a], 16)

            def exps(c, a):
                for k, unit in enumerate(KU):
                    g = 2 * c * NB + a * NB + k
                    width = sum(x[3] for x in unit)
                    act.wait_ge(key_scores, g + 1)
                    act.wait_ge(probs_used, g + 1)
                    nc.scalar.activation(probs[:, (a + k) % 2, 0:width], b_ps[(a + k) % 2][:, 0:width], ACT.Exp)\
                      .then_inc(probs_ready, 1)
                act.wait_ge(att_ready, 8 * c + 4 * a + 4)
                act.wait_ge(head_done, 2 * c + a + 5)
                for b in range(4):
                    nc.scalar.activation(staged[:, b, :], out_ps[:, 512 * b:512 * b + 512], ACT.Copy).then_inc(acc_copied, 1)

            rows(0, 0)
            rows(0, 1)
            exps(0, 0)

            def body(c, u, r):
                rows(c, 0)
                exps(c - 1, 1)
                rows(c, 1)
                exps(c, 0)

            later_pairs(act, body)
            exps(PAIRS - 1, 1)

        @block.tensor
        def _(pe):
            def maxima(c, u, a):
                q, kk = qT[:, u, :], kT[:, u, a, :]
                for k, unit in enumerate(QU):
                    bank = a_ps[k % 2]
                    width = sum(x[3] for x in unit)
                    pe.wait_ge(peaks_read, 2 * c * NA + a * NA + k + 1)
                    mask = masks[:, 0, 512 - width:512] if unit[-1][3] > P else masks[:, 1, 0:width]
                    nc.tensor.matmul(bank[:, 0:width], ident_bf[:], mask, start=True, stop=False)
                    at = 0
                    for p, m, first_key, n in unit:
                        d = DILATIONS[p]
                        last = nc.tensor.matmul(bank[:, at:at + n], tokens(q, d, m, P), tokens(kk, d, first_key, n),
                                                start=False, stop=(at + n == width))
                        at += n
                    last.then_inc(query_scores, 1)
                pe.wait_ge(peaks_read, 2 * c * NA + a * NA + NA + 1)
                nc.tensor.transpose(a_ps[(NA - 1) % 2][:, 0:P], peak[:, a, :], ident[:])\
                  .then_inc(query_scores, 1)

            def scores(c, u, a, k):
                q, kk = qT[:, u, :], kT[:, u, a, :]
                unit = KU[k]
                bank = b_ps[(a + k) % 2]
                width = sum(x[3] for x in unit)
                pe.wait_ge(probs_ready, 2 * c * NB + a * NB + k + 1)
                mask = masks[:, 2, 0:width] if unit[0][3] > P else masks[:, 3, 0:width]
                nc.tensor.matmul(bank[:, 0:width], ident_bf[:], mask, start=True, stop=False)
                at = 0
                for p, m, first_query, n in unit:
                    d = DILATIONS[p]
                    nc.tensor.matmul(bank[:, at:at + n], take_peak[:, a, :], tokens(peaks[:, a, :], d, first_query, n),
                                     start=False, stop=False)
                    last = nc.tensor.matmul(bank[:, at:at + n], tokens(kk, d, m, P), tokens(q, d, first_query, n),
                                            start=False, stop=(at + n == width))
                    at += n
                last.then_inc(key_scores, 1)

            def weigh(c, u, a, k):
                pe.wait_ge(probs_ready, 2 * c * NB + a * NB + k + 3)
                at = 0
                last = None
                for p, m, first_query, n in KU[k]:
                    d = DILATIONS[p]
                    v = v1[:, u, p, m, a * ATD:a * ATD + P]
                    s = tile_start(d, first_query)
                    done = 0
                    while done < n:
                        t = s + d * done
                        count = min(n - done, (512 - t % 512 + d - 1) // d)
                        last = nc.tensor.matmul(out_ps[:, t:t + d * (count - 1) + 1:d], v,
                                                probs[:, (a + k) % 2, at + done:at + done + count],
                                                start=False, stop=False,
                                                skip_group_check=True)
                        done += count
                    at += n
                last.then_inc(probs_used, 1)
                return last

            def head(c, u, a):
                pe.wait_ge(peak_lo_ready, 2 * c + a + 1)
                scores(c, u, a, 0)
                scores(c, u, a, 1)
                pe.wait_ge(acc_copied, 8 * c + 4 * a + 4)
                for b in range(4):
                    nc.tensor.matmul(out_ps[:, 512 * b:512 * b + 512], zeros[:], masks[0:1, 0, :], start=True, stop=False)
                for k in range(NB):
                    weigh(c, u, a, k)
                    if k + 2 < NB:
                        scores(c, u, a, k + 2)
                for b in range(4):
                    last = nc.tensor.matmul(out_ps[:, 512 * b:512 * b + 512], zeros[:], masks[0:1, 0, :],
                                            start=False, stop=True)
                last.then_inc(head_done, 1)

            pe.wait_ge(constants_ready, 2)
            pe.wait_ge(ones_ready, 8)

            pe.wait_ge(qk_loaded[0], 48)
            maxima(0, 0, 0)
            maxima(0, 0, 1)
            pe.wait_ge(v_loaded[0], 16 * V_LOADS)
            head(0, 0, 0)

            def body(c, u, r):
                pe.wait_ge(qk_loaded[u], 48 * r + 48)
                maxima(c, u, 0)
                head(c - 1, 1 - u, 1)
                maxima(c, u, 1)
                pe.wait_ge(v_loaded[u], 16 * V_LOADS * (r + 1))
                head(c, u, 0)

            later_pairs(pe, body)
            head(PAIRS - 1, (PAIRS - 1) % 2, 1)

        @block.vector
        def _(dve):
            def maxima(c, a):
                for k, unit in enumerate(QU):
                    dve.wait_ge(query_scores, 2 * c * NA + a * NA + k + 1)
                    bank = a_ps[k % 2]
                    at, runs = 0, []
                    for x in unit:
                        if runs and runs[-1][2] == x[3]:
                            runs[-1][3] += 1
                        else:
                            runs.append([at, x[0] * TILES + x[1], x[3], 1])
                        at += x[3]
                    for at, col, n, count in runs:
                        last = nc.vector.reduce_max(peak[:, a, col:col + count],
                                                    bank[:, at:at + n * count].rearrange("p (c n) -> p c n", n=n), axis=AX.X)
                    last.then_inc(peaks_read, 1)
                dve.wait_ge(query_scores, 2 * c * NA + (a + 1) * NA)
                dve.wait_ge(rows_loaded[a], 16 * c + 16)
                nc.vector.tensor_copy(peakT[:, a, :], a_ps[(NA - 1) % 2][0:3 * TILES, 0:P]).then_inc(peaks_read, 1)

            def rows(c, a):
                r = slice(32 * a, 32 * a + 1)
                dve.wait_ge(rows_loaded[a], 16 * c + 32)
                first, second, third = (peak_rows[r, p, :] for p in range(3))
                by4 = second.rearrange("o (b r i) -> o b i r", b=4, r=4)
                by16 = third.rearrange("o (m i) -> o i m", m=TILES)
                nc.vector.tensor_tensor(first.rearrange("o (b i r) -> o b i r", b=4, r=4),
                                        first.rearrange("o (b i r) -> o b i r", b=4, r=4), by4, ALU.max).then_inc(rows_max, 1)
                dve.wait_ge(rows_max, 4 * c + 2 * a + 1)
                nc.vector.tensor_tensor(first.rearrange("o (i m) -> o i m", m=TILES),
                                        first.rearrange("o (i m) -> o i m", m=TILES), by16, ALU.max).then_inc(rows_max, 1)
                dve.wait_ge(rows_max, 4 * c + 2 * a + 2)
                nc.vector.tensor_scalar(peaks[r, a, :], first, -1.0, None, ALU.mult).then_inc(peak_hi_ready, 1)
                dve.wait_ge(peak_hi_ready, 2 * c + a + 1)
                nc.vector.scalar_tensor_tensor(peaks[64 + 32 * a:65 + 32 * a, a, :], first, -1.0, peaks[r, a, :], ALU.mult, ALU.subtract)\
                  .then_inc(peak_lo_ready, 1)

            def normalize(c, a):
                mine, other = slice(a * ATD, (a + 1) * ATD), slice((1 - a) * ATD, (2 - a) * ATD)
                for b in range(4):
                    dve.wait_ge(acc_copied, 8 * c + 4 * a + b + 5)
                    nc.vector.reciprocal(denominator[mine, 512 * b:512 * b + 512], staged[other, b, :]).then_inc(den_ready, 1)
                dve.wait_ge(att_stored, 16 * c + 16)
                for b in range(4):
                    t = slice(512 * b, 512 * b + 512)
                    dve.wait_ge(den_ready, 8 * c + 4 * a + b + 1)
                    nc.vector.tensor_tensor(att[mine, t], staged[mine, b, :], denominator[mine, t], ALU.mult).then_inc(att_ready, 1)

            for a in range(2):
                nc.vector.memset(peakT[:, a, :], 0.0).then_inc(rows_loaded[a], 16)
            nc.vector.memset(att[:], 0.0).then_inc(att_stored, 16)
            nc.vector.memset(peak[:], 0.0).then_inc(peaks_read, 2)
            nc.vector.memset(probs[:], 0.0).then_inc(probs_used, 2)
            nc.vector.memset(denominator[:], 0.0).then_inc(probs_ready, 2)
            nc.vector.memset(peaks[:], 0.0).then_inc(head_done, 4)
            nc.vector.memset(zeros[:], 0.0).then_inc(att_ready, 4)
            nc.vector.memset(peak_rows[0:33, 0, 0:1], 0.0).then_inc(acc_copied, 4)
            dve.wait_ge(consts_in, 32)
            nc.vector.tensor_copy(masks[:], staged[:]).then_inc(constants_ready, 1)
            nc.vector.tensor_copy(ident_bf[:], ident[:]).then_inc(constants_ready, 1)

            maxima(0, 0)
            maxima(0, 1)
            rows(0, 0)
            rows(0, 1)

            def body(c, u, r):
                maxima(c, 0)
                normalize(c - 1, 0)
                rows(c, 0)
                maxima(c, 1)
                normalize(c - 1, 1)
                rows(c, 1)

            later_pairs(dve, body)
            normalize(PAIRS - 1, 0)
            normalize(PAIRS - 1, 1)


def sample_constants():
    heads = np.zeros((NS, ATW), np.float32)
    for h in range(ATH):
        heads[h, h * ATD:(h + 1) * ATD] = 1.0
    to_row = np.zeros((NS, NS, NS), np.float32)
    for b in range(NS):
        to_row[:, b, b] = 1.0
    return {"own_head": heads, "to_row": to_row}


SQ, SK, SF, SV, SG, SAQ, SAK, SAV = range(8)


def sample_mixer(nc, A, S):
    with ExitStack() as ctx:
        sb = lambda n, s, d=F32: ctx.enter_context(nc.sbuf_tensor(n, s, d))
        ps = lambda n, s: ctx.enter_context(nc.psum_tensor(n, s, F32))
        sem = semaphores(nc, ctx)
        NH = NS * ATH
        rows = sb("s_rows", [NS, 8, 512])
        ident = sb("ident3", [P, P])
        own_head = sb("own_head", [NS, ATW])
        to_row = sb("to_row", [NS, NS, NS])
        head_gain = sb("head_gain3", [P, HGH])
        state = sb("s_state", [P, NS, HGH, HGD])
        wide = sb("wide", [P, NS, HGW])
        aq_wide = sb("aq_wide", [P, NS, ATW])
        ak_wide = sb("ak_wide", [P, NS, ATW])
        av_row = sb("av_row", [1, NS, ATW])
        keys = sb("s_keys", [P, 2, NS, ATW])
        values = sb("s_values", [P, 3, NS, ATW])
        cols = sb("s_cols", [P, 3, HGH, NS])
        q_diag = sb("q_diag", [P, HGH, NS * NS])
        scores = sb("s_scores", [P, 4, NH])
        peak = sb("s_peak", [NH, 1])
        probs = sb("s_probs", [NH, 4 * P])
        den = sb("s_den", [NH, 1])
        probsT = sb("s_probsT", [P, 4, NH])
        picked = sb("s_picked", [NS, 2, ATW])
        cat = sb("s_cat", [NS, D])
        catT = sb("s_catT", [P, KT, NS])
        junk = sb("s_junk", [NS, HGD])
        o_sum, o_mean, o_guess, o_tmp, o_rstd = (sb(n, [NS, HGH]) for n in ("so_sum", "so_mean", "so_guess", "so_tmp", "so_rstd"))
        cols_ps = ps("cols_ps", [P, 3, HGH, NS])
        o_ps = ps("so_ps", [NS, HGW])
        sT_ps = ps("sT_ps", [NH, 4 * P])
        pT_ps = ps("pT_ps", [P, 4, NH])
        pv_ps = [ps(f"pv_ps{i}", [NS, ATW]) for i in range(2)]
        att_ps = ps("att_ps", [NS, ATW])
        catT_ps = ps("catT_ps", [P, KT, NS])

        aq_in, ak_in = sem("aq_in3"), sem("ak_in3")
        rows_in, state_in, wide_in, values_in, stored = (sem(n) for n in ("rows_in", "state_in", "wide_in", "values_in", "stored3"))
        keys_in = [sem(f"keys_in{p}") for p in range(3)]
        cols_filled, cols_ready, diag_ready, state_steps, state_done = (
            sem(n) for n in ("cols_filled", "cols_ready", "diag_ready", "state_steps", "state_done"))
        o_filled, o_squared, o_mean_ready, o_log, o_guessed, o_steps, o_rstd_ready, hn_steps = (
            sem(n) for n in ("so_filled", "so_squared", "so_mean_ready", "so_log", "so_guessed", "so_steps", "so_rstd_ready", "shn_steps"))
        products, score_ready, scoreT_filled, peak_steps, exp_done, prob_steps, probsT_filled, probsT_ready = (
            sem(n) for n in ("s_products", "s_score_ready", "s_scoreT_filled", "s_peak_steps", "s_exp_done", "s_prob_steps",
                             "s_probsT_filled", "s_probsT_ready"))
        pv_done, picked_ready, att_filled, cat_ready, catT_filled, catT_ready = (
            sem(n) for n in ("s_pv_done", "s_picked_ready", "s_att_filled", "s_cat_ready", "s_catT_filled", "s_catT_ready"))
        block = ctx.enter_context(nc.Block())

        def sample(c):
            return S["sample"][:, c * 512:(c + 1) * 512]

        def everywhere(c):
            return sample(c).unsqueeze(0).broadcast_to([P, NS, 512])

        def window(cache, d):
            return cache[0].rearrange("b w h e -> b w (h e)")[:, WIN - P * d:WIN, :]\
                .rearrange("b (j r) e -> j b r e", r=d)[:, :, 0, :]

        @block.sync
        def _(sp):
            sp.dma_start(rows[:], S["sample"].rearrange("b (c n) -> b c n", c=8)).then_inc(rows_in, 16)
            sp.dma_start(ident[:], A["ident"]).then_inc(rows_in, 16)
            sp.dma_start(own_head[:], A["own_head"]).then_inc(rows_in, 16)
            sp.dma_start(to_row[:], A["to_row"]).then_inc(rows_in, 16)
            sp.dma_start(head_gain[:], A["head_gain"]).then_inc(rows_in, 16)
            sp.dma_start(av_row[:], sample(SAV).unsqueeze(0)).then_inc(rows_in, 16)
            sp.dma_start(aq_wide[:], everywhere(SAQ)).then_inc(aq_in, 16)
            for p in range(2):
                sp.dma_start(keys[:, p], window(A["cache_attn_k"], DILATIONS[p])).then_inc(keys_in[p], 16)
            sp.dma_start(ak_wide[:], everywhere(SAK)).then_inc(ak_in, 16)
            sp.dma_start(state[:], A["state_hgrn"][0].rearrange("b h k v -> k b h v")).then_inc(state_in, 16)
            sp.dma_start(wide[:], everywhere(SV)).then_inc(wide_in, 16)
            sp.wait_ge(score_ready, 1)
            sp.dma_start(keys[:, 0], window(A["cache_attn_k"], DILATIONS[2])).then_inc(keys_in[2], 16)
            for p in range(3):
                sp.dma_start(values[:, p], window(A["cache_attn_v"], DILATIONS[p])).then_inc(values_in, 16)
            sp.dma_start(A["new_k_sample"][:, WIN - 1, :], sample(SAK)).then_inc(stored, 16)
            sp.dma_start(A["new_v_sample"][:, WIN - 1, :], sample(SAV)).then_inc(stored, 16)
            sp.wait_ge(state_done, 1)
            sp.dma_start(A["new_hgrn_sample"].rearrange("b h k v -> k b h v"), state[:]).then_inc(stored, 16)
            sp.wait_ge(catT_ready, 2)
            sp.dma_start(S["catT_sample"], catT[:]).then_inc(stored, 16)
            sp.wait_ge(stored, 64)

        @block.tensor
        def _(pe):
            pe.wait_ge(rows_in, 96)
            for c in range(3):
                for h in range(HGH):
                    last = nc.tensor.transpose(cols_ps[:, c, h, :], rows[:, c, h * HGD:(h + 1) * HGD], ident[0:NS, 0:NS])
            last.then_inc(cols_filled, 1)
            pe.wait_ge(diag_ready, 2)
            pe.wait_ge(state_done, 1)
            for h in range(HGH):
                for b in range(NS):
                    last = nc.tensor.matmul(o_ps[:, h * HGD:(h + 1) * HGD], q_diag[:, h, b * NS:(b + 1) * NS],
                                            state[:, b, h, :], start=(b == 0), stop=(b == NS - 1))
            last.then_inc(o_filled, 1)
            pe.wait_ge(score_ready, 4)
            for p in range(4):
                last = nc.tensor.transpose(sT_ps[:, p * P:(p + 1) * P], scores[:, p, :], ident[:])
            last.then_inc(scoreT_filled, 1)
            pe.wait_ge(prob_steps, 4)
            for p in range(4):
                last = nc.tensor.transpose(pT_ps[:, p, :], probs[:, p * P:(p + 1) * P], ident[0:NH, 0:NH])
            last.then_inc(probsT_filled, 1)
            pe.wait_ge(probsT_ready, 1)
            pe.wait_ge(values_in, 48)
            for b in range(NS + 1):
                if b < NS:
                    if b >= 2:
                        pe.wait_ge(picked_ready, b - 1)
                    hs = slice(b * ATH, (b + 1) * ATH)
                    for p in range(3):
                        nc.tensor.matmul(pv_ps[b % 2][:], probsT[:, p, hs], values[:, p, b, :], start=(p == 0), stop=False)
                    nc.tensor.matmul(pv_ps[b % 2][:], probsT[0:1, 3, hs], av_row[:, b, :], start=False, stop=True)\
                      .then_inc(pv_done, 1)
                if b >= 1:
                    pe.wait_ge(picked_ready, b)
                    last = nc.tensor.matmul(att_ps[:], to_row[:, b - 1, :], picked[:, (b - 1) % 2, :],
                                            start=(b == 1), stop=(b == NS))
            last.then_inc(att_filled, 1)
            pe.wait_ge(cat_ready, 1)
            pe.wait_ge(hn_steps, 2)
            for c in range(KT):
                last = nc.tensor.transpose(catT_ps[:, c, :], cat[:, c * P:(c + 1) * P], ident[0:NS, 0:NS])
            last.then_inc(catT_filled, 1)

        @block.scalar
        def _(act):
            act.wait_ge(o_filled, 1)
            for h in range(HGH):
                if h:
                    act.wait_ge(o_squared, h)
                nc.scalar.activation(junk[:], o_ps[:, h * HGD:(h + 1) * HGD], ACT.Square, accum_out=o_sum[:, h:h + 1])\
                  .then_inc(o_squared, 1)
            act.wait_ge(o_mean_ready, 1)
            guess_rsqrt(nc, act, o_guess[:], o_mean[:], o_log, 1, o_guessed)
            act.wait_ge(peak_steps, 3)
            nc.scalar.activation(probs[:, 0:3 * P + 1], sT_ps[:, 0:3 * P + 1], ACT.Exp, bias=peak[:]).then_inc(exp_done, 1)

        @block.gpsimd
        def _(pool):
            per_column = lambda c: cols[:, c].rearrange("p h b -> p b h").unsqueeze(3).broadcast_to([P, NS, HGH, HGD])
            v = wide[:].rearrange("p b (h e) -> p b h e", h=HGH)
            pool.wait_ge(cols_ready, 1)
            pool.wait_ge(state_in, 16)
            nc.gpsimd.tensor_tensor(state[:], state[:], per_column(2), ALU.mult).then_inc(state_steps, 1)
            pool.wait_ge(wide_in, 16)
            pool.wait_ge(state_steps, 1)
            nc.gpsimd.tensor_tensor(v, v, per_column(1), ALU.mult).then_inc(state_steps, 1)
            pool.wait_ge(state_steps, 2)
            nc.gpsimd.tensor_tensor(state[:], state[:], v, ALU.add).then_inc(state_done, 1)

        @block.vector
        def _(dve):
            nc.vector.memset(q_diag[:], 0.0).then_inc(diag_ready, 1)
            nc.vector.memset(probs[:], 0.0).then_inc(peak_steps, 1)
            dve.wait_ge(cols_filled, 1)
            nc.vector.tensor_copy(cols[:], cols_ps[:]).then_inc(cols_ready, 1)
            dve.wait_ge(cols_ready, 1)
            dve.wait_ge(diag_ready, 1)
            nc.vector.tensor_copy(q_diag[:, :, 0::NS + 1], cols[:, 0]).then_inc(diag_ready, 1)
            dve.wait_ge(aq_in, 16)
            for k, p in enumerate((0, 1, 3, 2)):
                dve.wait_ge(ak_in if p == 3 else keys_in[p], 16)
                product = keys[:, p % 2] if p < 3 else ak_wide[:]
                nc.vector.tensor_tensor(product, product, aq_wide[:], ALU.mult).then_inc(products, 1)
                dve.wait_ge(products, k + 1)
                nc.vector.reduce_sum(scores[:, p, :], product.rearrange("p b (h e) -> p (b h) e", e=ATD), axis=AX.X)\
                  .then_inc(score_ready, 1)
            dve.wait_ge(o_squared, HGH)
            nc.vector.tensor_scalar(o_mean[:], o_sum[:], 1.0 / HGD, EPS, ALU.mult, ALU.add).then_inc(o_mean_ready, 1)
            dve.wait_ge(o_guessed, 1)
            refine_rsqrt(nc, dve, o_rstd[:], o_guess[:], o_mean[:], o_tmp[:], o_steps, 0, o_rstd_ready)
            dve.wait_ge(o_rstd_ready, 1)
            nc.vector.tensor_tensor(cat[:, 0:HGW].rearrange("p (h e) -> p h e", h=HGH),
                                    o_ps[:].rearrange("p (h e) -> p h e", h=HGH),
                                    o_rstd[:].unsqueeze(2).broadcast_to([NS, HGH, HGD]), ALU.mult).then_inc(hn_steps, 1)
            dve.wait_ge(hn_steps, 1)
            nc.vector.tensor_tensor(cat[:, 0:HGW], cat[:, 0:HGW], rows[:, SG, :], ALU.mult).then_inc(hn_steps, 1)
            dve.wait_ge(scoreT_filled, 1)
            nc.vector.reduce_max(peak[:], sT_ps[:, 0:3 * P + 1], axis=AX.X).then_inc(peak_steps, 1)
            dve.wait_ge(peak_steps, 2)
            nc.vector.tensor_scalar(peak[:], peak[:], -1.0, None, ALU.mult).then_inc(peak_steps, 1)
            new = probs[:, 3 * P:3 * P + 1]
            dve.wait_ge(exp_done, 1)
            nc.vector.tensor_scalar(new, new, 3.0, None, ALU.mult).then_inc(prob_steps, 1)
            dve.wait_ge(prob_steps, 1)
            nc.vector.reduce_sum(den[:], probs[:, 0:3 * P + 1], axis=AX.X).then_inc(prob_steps, 1)
            dve.wait_ge(prob_steps, 2)
            nc.vector.reciprocal(den[:], den[:]).then_inc(prob_steps, 1)
            dve.wait_ge(prob_steps, 3)
            nc.vector.tensor_scalar(probs[:, 0:3 * P + 1], probs[:, 0:3 * P + 1], den[:], None, ALU.mult).then_inc(prob_steps, 1)
            dve.wait_ge(probsT_filled, 1)
            nc.vector.tensor_copy(probsT[:], pT_ps[:]).then_inc(probsT_ready, 1)
            for b in range(NS):
                dve.wait_ge(pv_done, b + 1)
                nc.vector.tensor_tensor(picked[:, b % 2, :], pv_ps[b % 2][:], own_head[:], ALU.mult).then_inc(picked_ready, 1)
            dve.wait_ge(att_filled, 1)
            nc.vector.tensor_copy(cat[:, HGW:], att_ps[:]).then_inc(cat_ready, 1)
            dve.wait_ge(catT_filled, 1)
            nc.vector.tensor_tensor(catT[:, 0:HGH, :], catT_ps[:, 0:HGH, :],
                                    head_gain[:].unsqueeze(2).broadcast_to([P, HGH, NS]), ALU.mult).then_inc(catT_ready, 1)
            nc.vector.tensor_copy(catT[:, HGH:, :], catT_ps[:, HGH:, :]).then_inc(catT_ready, 1)


NT = TILES + 1


def routing_constants():
    t = np.arange(P)
    real = np.zeros((P, 1), np.float32)
    real[:NS] = 1.0
    return {"iota": np.tile(np.arange(EXPERTS, dtype=np.float32), (P, 1)), "real_row": real,
            "before": (t[:, None] < t[None]).astype(np.float32),
            "row_number": t[:, None].astype(np.float32)}


def tile_turns(eng, body):
    body(0, 0, 0, past=0)
    body(1, 1, 0, past=1)
    with eng.Fori(0, (TILES - 2) // 2) as i:
        for u in range(2):
            body(2 * i + 2 + u, u, i + 1, past=2)
    body(TILES, 0, TILES // 2, past=2)


def project_out_and_route(nc, A, S, R):
    with ExitStack() as ctx:
        sb = lambda n, s, d=F32: ctx.enter_context(nc.sbuf_tensor(n, s, d))
        ps = lambda n, s: ctx.enter_context(nc.psum_tensor(n, s, F32))
        sem = semaphores(nc, ctx)
        w_out = sb("w_out", [P, KT, D])
        w_route = sb("w_route", [P, KT, GROUPS + EXPERTS])
        ident = sb("ident4", [P, P])
        ffn_gain = sb("ffn_gain4", [P, KT])
        iota = sb("iota4", [P, EXPERTS])
        real_row = sb("real_row", [P, 1])
        catT = [sb(f"catT{i}", [P, KT, P]) for i in range(3)]
        xr = [sb(f"xr{i}", [P, D]) for i in range(3)]
        h2 = sb("h2", [P, 2, D])
        h2T = sb("h2T", [P, KT, P])
        junk = sb("junk4", [P, D], BF16)
        square_sum, mean, guess, tmp, rstd = (sb(n, [P, 1]) for n in ("ssq4", "mean4", "guess4", "tmp4", "rstd4"))
        carrier = sb("carrier4", [1, 1])
        logits = sb("logits", [P, GROUPS + EXPERTS])
        top_g, top_e = sb("top_g", [P, 8]), sb("top_e", [P, 8])
        at_g, at_e = sb("at_g", [P, 8], U32), sb("at_e", [P, 8], U32)
        neg_top, group_exp, group_sum, p_group = sb("neg_top", [P, 1]), sb("group_exp", [P, 8]), sb("group_sum", [P, 1]), sb("p_group", [P, 1])
        group_at, in_group = sb("group_at", [P, 1]), sb("in_group", [P, GROUPS])
        group_logits, own_logits = sb("group_logits", [P, GROUPS, PER_GROUP]), sb("own_logits", [P, PER_GROUP])
        behind, ratio, share = sb("behind", [P, 1]), sb("ratio", [P, 1]), sb("share", [P, 1])
        expert_at, first_of_group, expert = sb("expert_at", [P, 2]), sb("first_of_group", [P, 1]), sb("expert", [P, 2])
        o_ps = [ps(f"o_ps4{i}", [P, 512]) for i in range(2)]
        t_ps = [ps(f"t_ps4{i}", [P, 4, P]) for i in range(2)]
        l_ps = ps("l_ps", [P, GROUPS + EXPERTS])

        consts_in, w_out_in, zeroed = sem("consts_in4"), sem("w_out_in"), sem("zeroed4")
        cat_in = [sem(f"cat_in{u}") for u in range(2)]
        x_in = [sem(f"x_in{u}") for u in range(2)]
        res_stored = [sem(f"res_stored{u}") for u in range(2)]
        h_stored = [sem(f"h_stored{u}") for u in range(2)]
        o_done, x1_ready, squared, mean_ready, logged, guessed, steps, rstd_ready, h2_ready = (
            sem(n + "4") for n in ("o_done", "x1_ready", "squared", "mean_ready", "logged", "guessed", "steps",
                                   "rstd_ready", "h2_ready"))
        h2T_filled, h2T_ready, logits_done, logits_ready = (
            sem(n + "4") for n in ("h2T_filled", "h2T_ready", "logits_done", "logits_ready"))
        neg_ready, group_exp_ready, behind_ready, ratio_ready = (
            sem(n + "4") for n in ("neg_ready", "group_exp_ready", "behind_ready", "ratio_ready"))
        route = sem("route_steps4")
        ROUTE_STEPS = 20
        block = ctx.enter_context(nc.Block())

        def buffers(n, u):
            return (catT[2], xr[2]) if isinstance(n, int) and n == TILES else (catT[u], xr[u])

        @block.sync
        def _(sp):
            sp.dma_start(w_out[:], A["w_out"][0].rearrange("(t p) n -> p t n", p=P)).then_inc(w_out_in, 16)

            def store(n, u):
                x1 = buffers(n, u)[1]
                sp.wait_ge(x1_ready, 2 * n + 2)
                sp.wait_ge(h2_ready, n + 1)
                sp.dma_start(S["res"][bass.ds(n * P, P), :], x1[:]).then_inc(res_stored[u], 16)
                sp.dma_start(S["hrows"][bass.ds(n * P, P), :], h2[:, u, :]).then_inc(h_stored[u], 16)

            def body(n, u, r, past):
                cT, x = buffers(n, u)
                if isinstance(n, int) and n == TILES:
                    sp.wait_ge(zeroed, 2)
                    sp.dma_start(cT[:, :, 0:NS], S["catT_sample"]).then_inc(cat_in[u], 16)
                    sp.dma_start(x[0:NS, :], A["x_sample"][:, 0, :]).then_inc(x_in[u], 16)
                else:
                    if past == 2:
                        sp.wait_ge(o_done, 2 * n - 2)
                        sp.wait_ge(res_stored[u], 16 * r)
                    sp.dma_start(cT[:], S["catT"][:, :, bass.ds(n * P, P)].rearrange("c p t -> p c t")).then_inc(cat_in[u], 16)
                    sp.dma_start(x[:], A["x_prompt"][0, bass.ds(n * P, P), :]).then_inc(x_in[u], 16)
                if past:
                    store(n - 1, 1 - u)

            tile_turns(sp, body)
            store(TILES, 0)
            for u in range(2):
                sp.wait_ge(res_stored[u], 16 * (TILES // 2 + 1 - u))
                sp.wait_ge(h_stored[u], 16 * (TILES // 2 + 1 - u))

        @block.tensor
        def _(pe):
            def post(m, v, past):
                pe.wait_ge(h2_ready, m + 1)
                for half in range(2):
                    if past:
                        pe.wait_ge(h2T_ready, 2 * m - 1 + half)
                    for c in range(4):
                        k = 4 * half + c
                        last = nc.tensor.transpose(t_ps[half][:, c, :], h2[:, v, k * P:(k + 1) * P], ident[:])
                    last.then_inc(h2T_filled, 1)
                pe.wait_ge(h2T_ready, 2 * m + 2)
                if past:
                    pe.wait_ge(logits_ready, m)
                for c in range(KT):
                    last = nc.tensor.matmul(l_ps[:], h2T[:, c, :], w_route[:, c, :], start=(c == 0), stop=(c == KT - 1))
                last.then_inc(logits_done, 1)

            pe.wait_ge(consts_in, 16 * (5 + GROUPS))
            pe.wait_ge(w_out_in, 16)

            def body(n, u, r, past):
                cT = buffers(n, u)[0]
                pe.wait_ge(cat_in[u], 16 * r + 16)
                for half in range(2):
                    if past:
                        pe.wait_ge(x1_ready, 2 * n - 1 + half)
                    for c in range(KT):
                        last = nc.tensor.matmul(o_ps[half][:], cT[:, c, :], w_out[:, c, half * 512:half * 512 + 512],
                                                start=(c == 0), stop=(c == KT - 1))
                    last.then_inc(o_done, 1)
                if past:
                    post(n - 1, 1 - u, past - 1)

            tile_turns(pe, body)
            post(TILES, 0, 1)

        @block.scalar
        def _(act):
            for dst, src in ((ident, A["ident"]), (ffn_gain, A["ffn_gain"]), (iota, A["iota"]), (real_row, A["real_row"])):
                act.dma_start(dst[:], src).then_inc(consts_in, 16)
            act.dma_start(w_route[:, :, 0:GROUPS], A["w_route_group"][0].rearrange("(t p) g -> p t g", p=P)).then_inc(consts_in, 16)
            for g in range(GROUPS):
                c = GROUPS + g * PER_GROUP
                act.dma_start(w_route[:, :, c:c + PER_GROUP], A["w_route_expert"][0, g].rearrange("(t p) e -> p t e", p=P))\
                   .then_inc(consts_in, 16)

            def body(n, u, r, past):
                x1 = buffers(n, u)[1]
                act.wait_ge(x1_ready, 2 * n + 2)
                if past:
                    act.wait_ge(rstd_ready, n)
                nc.scalar.activation(junk[:], x1[:], ACT.Square, accum_out=square_sum[:]).then_inc(squared, 1)
                act.wait_ge(mean_ready, n + 1)
                guess_rsqrt(nc, act, guess[:], mean[:], logged, n + 1, guessed)
                act.wait_ge(rstd_ready, n + 1)
                if past == 2:
                    act.wait_ge(h_stored[u], 16 * r)
                nc.scalar.activation(h2[:, u, :], x1[:], ACT.Copy, scale=rstd[:]).then_inc(h2_ready, 1)
                if past:
                    gates(n - 1)

            def gates(m):
                act.wait_ge(neg_ready, m + 1)
                nc.scalar.activation(group_exp[:], logits[:, 0:GROUPS], ACT.Exp, bias=neg_top[:], accum_out=group_sum[:])\
                  .then_inc(group_exp_ready, 1)
                act.wait_ge(behind_ready, m + 1)
                nc.scalar.activation(ratio[:], behind[:], ACT.Exp).then_inc(ratio_ready, 1)

            tile_turns(act, body)
            gates(TILES)

        @block.vector
        def _(dve):
            def routing(m, past):
                count = [0]

                def step(instruction, waits=True):
                    count[0] += 1
                    instruction.then_inc(route, 1)
                    if waits:
                        dve.wait_ge(route, ROUTE_STEPS * m + count[0])

                dve.wait_ge(logits_done, m + 1)
                nc.vector.tensor_copy(logits[:], l_ps[:]).then_inc(logits_ready, 1)
                dve.wait_ge(logits_ready, m + 1)
                nc.vector.memset(carrier[:], 0.0)
                step(nc.vector.max(top_g[:], logits[:, 0:GROUPS]))
                nc.vector.tensor_scalar(neg_top[:], top_g[:, 0:1], -1.0, None, ALU.mult).then_inc(neg_ready, 1)
                step(nc.vector.max_index(at_g[:], top_g[:], logits[:, 0:GROUPS]))
                step(nc.vector.tensor_copy(group_at[:], at_g[:, 0:1]))
                step(nc.vector.tensor_scalar(first_of_group[:], group_at[:], float(PER_GROUP), None, ALU.mult), False)
                step(nc.vector.tensor_scalar(in_group[:], iota[:, 0:GROUPS], group_at[:], None, ALU.is_equal))
                step(nc.vector.tensor_tensor(group_logits[:], logits[:, GROUPS:].rearrange("p (g e) -> p g e", g=GROUPS),
                                             in_group[:].unsqueeze(2).broadcast_to([P, GROUPS, PER_GROUP]), ALU.mult))
                step(nc.vector.reduce_sum(own_logits[:], group_logits[:].rearrange("p g e -> p e g"), axis=AX.X), False)
                dve.wait_ge(route, ROUTE_STEPS * m + count[0])
                nc.vector.memset(carrier[:], 0.0)
                step(nc.vector.max(top_e[:], own_logits[:]))
                nc.vector.tensor_tensor(behind[:], top_e[:, 1:2], top_e[:, 0:1], ALU.subtract).then_inc(behind_ready, 1)
                step(nc.vector.max_index(at_e[:], top_e[:], own_logits[:]))
                step(nc.vector.tensor_copy(expert_at[:], at_e[:, 0:2]))
                step(nc.vector.tensor_scalar(expert[:], expert_at[:], first_of_group[:], None, ALU.add))
                for k in range(2):
                    step(nc.vector.tensor_scalar(R["chosen"][k][:, bass.ds(m, 1), :], iota[:].unsqueeze(1),
                                                 expert[:, k:k + 1], None, ALU.is_equal), False)
                dve.wait_ge(group_exp_ready, m + 1)
                dve.wait_ge(ratio_ready, m + 1)
                step(nc.vector.reciprocal(p_group[:], group_sum[:]), False)
                step(nc.vector.tensor_scalar(share[:], ratio[:], 1.0, None, ALU.add))
                step(nc.vector.reciprocal(share[:], share[:]))
                gate = lambda k: R["gates"][:, bass.ds(m, 1), k]
                step(nc.vector.tensor_tensor(gate(0), share[:], p_group[:], ALU.mult))
                step(nc.vector.tensor_tensor(gate(1), gate(0), ratio[:], ALU.mult))
                for _ in range(ROUTE_STEPS - count[0]):
                    step(nc.vector.memset(share[:], 0.0))

            nc.vector.memset(catT[2][:], 0.0).then_inc(zeroed, 1)
            nc.vector.memset(xr[2][:], 0.0).then_inc(zeroed, 1)
            dve.wait_ge(consts_in, 16 * (5 + GROUPS))

            def drains(m):
                for half in range(2):
                    dve.wait_ge(h2T_filled, 2 * m + half + 1)
                    gain = ffn_gain[:, 4 * half:4 * half + 4].unsqueeze(2).broadcast_to([P, 4, P])
                    nc.vector.tensor_tensor(h2T[:, 4 * half:4 * half + 4, :], t_ps[half][:], gain, ALU.mult).then_inc(h2T_ready, 1)

            def body(n, u, r, past):
                x = buffers(n, u)[1]
                dve.wait_ge(x_in[u], 16 * r + 16)
                for half in range(2):
                    dve.wait_ge(o_done, 2 * n + half + 1)
                    c = slice(half * 512, half * 512 + 512)
                    nc.vector.tensor_tensor(x[:, c], o_ps[half][:], x[:, c], ALU.add).then_inc(x1_ready, 1)
                if past:
                    drains(n - 1)
                dve.wait_ge(squared, n + 1)
                nc.vector.tensor_scalar(mean[:], square_sum[:], 1.0 / D, EPS, ALU.mult, ALU.add).then_inc(mean_ready, 1)
                dve.wait_ge(guessed, n + 1)
                if past:
                    dve.wait_ge(h2_ready, n)
                refine_rsqrt(nc, dve, rstd[:], guess[:], mean[:], tmp[:], steps, 3 * n, rstd_ready)
                if past:
                    routing(n - 1, past - 1)

            tile_turns(dve, body)
            drains(TILES)
            routing(TILES, 1)
            for k in range(2):
                dve.wait_ge(route, ROUTE_STEPS * NT)
                nc.vector.tensor_scalar(R["chosen"][k][:, TILES, :], R["chosen"][k][:, TILES, :], real_row[:], None, ALU.mult)\
                  .then_inc(route, 1)
            dve.wait_ge(route, ROUTE_STEPS * NT + 2)


def load_expert(eng, A, name, dst, expert, arrived):
    eng.dma_start(dst, A[name][0, bass.ds(expert, 1), :, :].rearrange("o (t p) n -> p (o t) n", p=P)).then_inc(arrived, 16)


def assign_slots(nc, A, S, R, W):
    with ExitStack() as ctx:
        sb = lambda n, s, d=F32: ctx.enter_context(nc.sbuf_tensor(n, s, d))
        ps = lambda n, s: ctx.enter_context(nc.psum_tensor(n, s, F32))
        sem = semaphores(nc, ctx)
        before, ident, row_number = sb("before", [P, P]), sb("ident5", [P, P]), sb("row_number", [P, 1])
        before_bf, ones_bf = sb("before_bf", [P, P], BF16), sb("ones_bf", [P, P], BF16)
        taken = sb("taken", [P, NT, EXPERTS], BF16)
        so_far = sb("so_far", [P, NT + 1, EXPERTS], BF16)
        count, count_i = sb("count", [P, EXPERTS]), sb("count_i", [P, EXPERTS], I32)
        blocks, through, first, ones = (sb(n, [P, EXPERTS]) for n in ("blocks", "through", "first_slot", "ones5"))
        place = sb("place", [P, NT, EXPERTS])
        chosen_place = sb("chosen_place", [P, NT, EXPERTS])
        slot_f = sb("slot_f", [P, 2, NT])
        passed, expert_of = sb("passed", [P, EXPERTS]), sb("expert_of", [P, 1])
        token = sb("token", [P, NT], I32)
        zero_table = sb("zero_table", [SLOT_BLOCKS, P], I32)
        table, table_f = sb("table", [SLOT_BLOCKS, P], I32), sb("table_f", [SLOT_BLOCKS, P])
        rank_ps = [ps(f"rank_ps{i}", [P, 8, EXPERTS]) for i in range(3)]
        count_ps, expert_ps, table_ps = ps("count_ps", [P, EXPERTS]), ps("expert_ps", [1, P]), ps("table_ps", [P, SLOT_BLOCKS])
        consts_in, token_ready, table_zeroed, scattered, table_in = (
            sem(n + "5") for n in ("consts_in", "token_ready", "table_zeroed", "scattered", "table_in"))
        step, ranked, counted, experts_done, tableT_done, slots_ready, zero_ready, table_float = (
            sem(n + "5") for n in ("step", "ranked", "counted", "experts_done", "tableT_done", "slots_ready", "zero_ready", "table_float"))
        experts_known, weights_in = sem("experts_known5"), sem("weights_in5")
        expert_ready, taken_ready = sem("expert_ready5"), sem("taken_ready5")
        block = ctx.enter_context(nc.Block())

        @block.sync
        def _(sp):
            for dst, src in ((before, A["before"]), (ident, A["ident"]), (row_number, A["row_number"])):
                sp.dma_start(dst[:], src).then_inc(consts_in, 16)
            sp.wait_ge(zero_ready, 1)
            sp.dma_start(S["slot_token"].rearrange("(a b) o -> a (b o)", b=P), zero_table[:]).then_inc(table_zeroed, 16)
            sp.wait_ge(experts_known, 1)
            first, second = (sp.value_load(R["block_expert"][0:1, b:b + 1], min_val=0, max_val=EXPERTS - 1) for b in range(2))
            load_expert(sp, A, "w_expert_gate", W["gate"][:, 0], first, weights_in)
            load_expert(sp, A, "w_expert_up", W["up"][:, 0], first, weights_in)
            load_expert(sp, A, "w_expert_gate", W["gate"][:, 1], second, weights_in)
            load_expert(sp, A, "w_expert_up", W["up"][:, 1], second, weights_in)
            load_expert(sp, A, "w_expert_down", W["down"][:, 0], first, weights_in)
            sp.wait_ge(scattered, 16 * 2 * NT)
            sp.dma_start(table[:], S["slot_token"].rearrange("(a b) o -> a (b o)", b=P)).then_inc(table_in, 16)
            sp.wait_ge(weights_in, 16 * 5)

        @block.gpsimd
        def _(pool):
            nc.gpsimd.iota(token[:], [[P, NT]], base=0, channel_multiplier=1).then_inc(token_ready, 1)
            pool.wait_ge(token_ready, 1)
            pool.wait_ge(table_zeroed, 16)
            for k in range(2):
                pool.wait_ge(slots_ready, k + 1)
                for n in range(NT):
                    rows = NS if n == TILES else P
                    pool.indirect_dma_start(
                        out=S["slot_token"], out_offset=bass.IndirectOffsetOnAxis(ap=R["slots"][0:rows, k, n:n + 1], axis=0),
                        in_=token[0:rows, n:n + 1], in_offset=None).then_inc(scattered, 16)

        @block.tensor
        def _(pe):
            pe.wait_ge(taken_ready, 4 + NT)
            pe.wait_ge(step, 1)
            pe.wait_ge(consts_in, 48)
            for n in range(NT):
                out = rank_ps[n // 8][:, n % 8, :]
                nc.tensor.matmul(out, before_bf[:], taken[:, n, :], start=True, stop=False)
                last = nc.tensor.matmul(out, ones_bf[:], so_far[:, n, :], start=False, stop=True)
            last.then_inc(ranked, 1)
            nc.tensor.matmul(count_ps[:], ones_bf[:], so_far[:, NT, :], start=True, stop=True).then_inc(counted, 1)
            pe.wait_ge(expert_ready, 1)
            nc.tensor.matmul(expert_ps[:], expert_of[:], ident[:], start=True, stop=True).then_inc(experts_done, 1)
            pe.wait_ge(table_float, 1)
            nc.tensor.matmul(table_ps[:], table_f[:], ident[0:SLOT_BLOCKS, 0:SLOT_BLOCKS], start=True, stop=True)\
              .then_inc(tableT_done, 1)

        @block.vector
        def _(dve):
            at = [0]

            def chain(instruction):
                at[0] += 1
                instruction.then_inc(step, 1)
                dve.wait_ge(step, at[0])

            nc.vector.memset(zero_table[:], 0).then_inc(zero_ready, 1)
            nc.vector.memset(ones[:], 1.0).then_inc(taken_ready, 1)
            nc.vector.memset(ones_bf[:], 1.0).then_inc(taken_ready, 1)
            nc.vector.tensor_tensor(taken[:], R["chosen"][0][:], R["chosen"][1][:], ALU.add).then_inc(taken_ready, 1)
            nc.vector.memset(so_far[:, 0, :], 0.0).then_inc(taken_ready, 1)
            for n in range(NT):
                dve.wait_ge(taken_ready, 4 + n)
                nc.vector.tensor_tensor(so_far[:, n + 1, :], so_far[:, n, :], taken[:, n, :], ALU.add).then_inc(taken_ready, 1)
            dve.wait_ge(consts_in, 48)
            chain(nc.vector.tensor_copy(before_bf[:], before[:]))
            dve.wait_ge(counted, 1)
            chain(nc.vector.tensor_scalar(count[:], count_ps[:], float(P - 1), None, ALU.add))
            chain(nc.vector.tensor_copy(count_i[:], count[:]))
            chain(nc.vector.tensor_single_scalar(count_i[:], count_i[:], 7, ALU.logical_shift_right))
            chain(nc.vector.tensor_copy(blocks[:], count_i[:]))
            chain(nc.vector.tensor_tensor_scan(through[:], ones[:], blocks[:], 0.0, ALU.mult, ALU.add))
            chain(nc.vector.tensor_tensor(first[:], through[:], blocks[:], ALU.subtract))
            chain(nc.vector.tensor_scalar(first[:], first[:], float(P), None, ALU.mult))
            chain(nc.vector.tensor_scalar(passed[:], through[:], row_number[:], None, ALU.is_le))
            chain(nc.vector.reduce_sum(expert_of[:], passed[:], axis=AX.X))
            nc.vector.tensor_scalar(expert_of[:], expert_of[:], float(EXPERTS - 1), None, ALU.min).then_inc(expert_ready, 1)
            dve.wait_ge(ranked, 1)
            for i in range(3):
                n = min(8, NT - 8 * i)
                last = nc.vector.tensor_tensor(place[:, 8 * i:8 * i + n, :], rank_ps[i][:, 0:n, :],
                                               first[:].unsqueeze(1).broadcast_to([P, n, EXPERTS]), ALU.add)
                chain(last)
            for k in range(2):
                chain(nc.vector.tensor_tensor(chosen_place[:], place[:], R["chosen"][k][:], ALU.mult))
                chain(nc.vector.reduce_sum(slot_f[:, k, :], chosen_place[:], axis=AX.X))
                nc.vector.tensor_copy(R["slots"][:, k, :], slot_f[:, k, :]).then_inc(slots_ready, 1)
            dve.wait_ge(experts_done, 1)
            nc.vector.tensor_copy(R["block_expert"][:, 0:P], expert_ps[:]).then_inc(experts_known, 1)
            chain(nc.vector.tensor_copy(R["block_expert"][:, P:P + 1], through[0:1, EXPERTS - 1:EXPERTS]))
            pairs = R["block_expert"][:, P:P + 1]
            chain(nc.vector.tensor_single_scalar(pairs, pairs, 1, ALU.logical_shift_right))
            dve.wait_ge(table_in, 16)
            nc.vector.tensor_copy(table_f[:], table[:]).then_inc(table_float, 1)
            dve.wait_ge(tableT_done, 1)
            chain(nc.vector.tensor_copy(R["token_of"][:], table_ps[:]))


def experts(nc, A, S, R, W):
    with ExitStack() as ctx:
        sb = lambda n, s, d=F32: ctx.enter_context(nc.sbuf_tensor(n, s, d))
        ps = lambda n, s: ctx.enter_context(nc.psum_tensor(n, s, F32))
        sem = semaphores(nc, ctx)
        FT = FF // P
        w_gate, w_up, w_down = W["gate"], W["up"], W["down"]
        ident, ffn_gain = sb("ident6", [P, P]), sb("ffn_gain6", [P, KT])
        index = sb("index", [P, 2], I32)
        rows = [sb(f"rows{u}", [P, D]) for u in range(2)]
        xT = sb("xT6", [P, 2, KT, P])
        exp_g, sig = sb("exp_g6", [P, FF]), sb("sig6", [P, FF])
        hidden, hiddenT = sb("hidden", [P, FF]), sb("hiddenT", [P, FT, P])
        y = sb("y6", [P, 2, D])
        lead = sb("lead6", [1, 18])
        g_ps = [ps(f"g_ps{u}", [P, FF]) for u in range(2)]
        u_ps = ps("u_ps", [P, FF])
        t_ps = [ps(f"t_ps6{i}", [P, 4, P]) for i in range(2)]
        h_ps = ps("h_ps", [P, FT, P])
        y_ps = [ps(f"y_ps{i}", [P, 512]) for i in range(2)]
        consts_in = sem("consts_in6")
        gate_in, up_in, down_in, rows_in, y_stored = ([sem(f"{n}6{u}") for u in range(2)] for n in
                                                      ("gate_in", "up_in", "down_in", "rows_in", "y_stored"))
        gate_done, up_done, down_done = sem("gate_done6"), sem("up_done6"), sem("down_done6")
        index_ready, xT_filled, xT_ready = sem("index_ready6"), sem("xT_filled6"), sem("xT_ready6")
        exp_ready, sig_steps, hidden_ready, hidden_filled, hiddenT_ready = (
            sem(n + "6") for n in ("exp_ready", "sig_steps", "hidden_ready", "hidden_filled", "hiddenT_ready"))
        carried = sem("carried6")
        carrier = sb("carrier6", [1, 1])
        y_low, y_high = sem("y_low6"), sem("y_high6")
        block = ctx.enter_context(nc.Block())

        def pairs(eng):
            return eng.value_load(R["block_expert"][0:1, P:P + 1], min_val=2, max_val=(OUT_BLOCKS - 1) // 2)

        def blocks(eng, body):
            body(0, 0, 0, True)
            n = pairs(eng)
            with eng.Fori(0, n) as i:
                body(2 * i + 1, 1, i, False)
                body(2 * i + 2, 0, i + 1, False)
            return n

        @block.sync
        def _(sp):
            sp.dma_start(ident[:], A["ident"]).then_inc(consts_in, 16)
            sp.dma_start(ffn_gain[:], A["ffn_gain"]).then_inc(consts_in, 16)

            expert_of = lambda b: sp.value_load(R["block_expert"][0:1, bass.ds(b, 1)], min_val=0, max_val=EXPERTS - 1)

            def body(b, u):
                own, before = expert_of(b), expert_of(b - 1)
                sp.wait_ge(gate_done, b + 1)
                load_expert(sp, A, "w_expert_gate", w_gate[:, u], own, gate_in[u])
                sp.wait_ge(up_done, b + 1)
                load_expert(sp, A, "w_expert_up", w_up[:, u], own, up_in[u])
                sp.wait_ge(down_done, b)
                load_expert(sp, A, "w_expert_down", w_down[:, 1 - u], before, down_in[1 - u])

            n = pairs(sp)
            with sp.Fori(0, n - 1) as i:
                body(2 * i + 2, 0)
                body(2 * i + 3, 1)
            body(2 * n, 0)
            last = expert_of(2 * n)
            sp.wait_ge(down_done, 2 * n + 1)
            load_expert(sp, A, "w_expert_down", w_down[:, 0], last, down_in[0])

        @block.gpsimd
        def _(pool):
            def gather(b, u):
                pool.wait_ge(index_ready, b + 1)
                pool.wait_ge(xT_filled, 2 * b + 2)
                pool.wait_ge(carried, b + 1)
                nc.gpsimd.tensor_tensor(carrier[:], lead[:, 9:10], lead[:, 9:10], ALU.add).then_inc(carried, 1)
                pool.indirect_dma_start(out=rows[u][:], out_offset=None, in_=S["hrows"],
                                        in_offset=bass.IndirectOffsetOnAxis(ap=index[:, u:u + 1], axis=0))\
                    .then_inc(rows_in[u], 16)

            gather(0, 0)
            gather(1, 1)
            blocks(pool, lambda b, u, r, first: gather(b + 2, u))

        @block.scalar
        def _(act):
            def leave(b, u, r):
                act.wait_ge(down_done, b + 3)
                act.wait_ge(y_stored[u], 16 * r + 16)
                nc.scalar.activation(y[:, u, 0:512], y_ps[0][:], ACT.Copy).then_inc(y_low, 1)
                act.wait_ge(y_low, b + 2)
                act.wait_ge(y_high, b + 2)
                act.dma_start(S["y_slots"][bass.ds(b * P, P), :], y[:, u, :]).then_inc(y_stored[u], 16)

            def body(b, u, r, first):
                act.wait_ge(gate_done, b + 3)
                act.wait_ge(hidden_ready, b + 1)
                nc.scalar.activation(exp_g[:], g_ps[u][:], ACT.Exp, scale=-1.0).then_inc(exp_ready, 1)
                if not first:
                    leave(b - 1, 1 - u, r - 1 + u)

            n = blocks(act, body)
            leave(2 * n, 0, n)
            act.wait_ge(y_stored[0], 16 * n + 32)
            act.wait_ge(y_stored[1], 16 * n + 16)
            act.wait_ge(rows_in[0], 16 * n + 32)
            act.wait_ge(rows_in[1], 16 * n + 16)
            nc.scalar.activation(lead[:, 17:18], lead[:, 10:11], ACT.Copy)

        @block.tensor
        def _(pe):
            def transpose_rows(b, u, r):
                pe.wait_ge(rows_in[u], 16 * r + 16)
                for half in range(2):
                    for c in range(4):
                        k = 4 * half + c
                        last = nc.tensor.transpose(t_ps[half][:, c, :], rows[u][:, k * P:(k + 1) * P], ident[:])
                    last.then_inc(xT_filled, 1)

            def gate(b, u, r):
                pe.wait_ge(xT_ready, 2 * b + 2)
                pe.wait_ge(gate_in[u], 16 * r + 16)
                for c in range(KT):
                    last = nc.tensor.matmul(g_ps[u][:], xT[:, u, c, :], w_gate[:, u, c, :], start=(c == 0), stop=(c == KT - 1))
                last.then_inc(gate_done, 1)

            def up(b, u, r):
                pe.wait_ge(up_in[u], 16 * r + 16)
                pe.wait_ge(hidden_ready, b + 1)
                for c in range(KT):
                    last = nc.tensor.matmul(u_ps[:], xT[:, u, c, :], w_up[:, u, c, :], start=(c == 0), stop=(c == KT - 1))
                last.then_inc(up_done, 1)

            def transpose_hidden(b):
                pe.wait_ge(hidden_ready, b + 2)
                for c in range(FT):
                    last = nc.tensor.transpose(h_ps[:, c, :], hidden[:, c * P:(c + 1) * P], ident[:])
                last.then_inc(hidden_filled, 1)

            def down(b, u, r):
                pe.wait_ge(hiddenT_ready, b + 2)
                pe.wait_ge(down_in[u], 16 * r + 16)
                pe.wait_ge(y_low, b + 1)
                pe.wait_ge(y_high, b + 1)
                for half in range(2):
                    for c in range(FT):
                        last = nc.tensor.matmul(y_ps[half][:], hiddenT[:, c, :], w_down[:, u, c, half * 512:half * 512 + 512],
                                                start=(c == 0), stop=(c == FT - 1))
                last.then_inc(down_done, 1)

            def body(b, u, r, first):
                gate(b, u, r)
                if not first:
                    transpose_hidden(b - 1)
                transpose_rows(b + 1, 1 - u, r + u)
                up(b, u, r)
                if not first:
                    down(b - 1, 1 - u, r - 1 + u)

            pe.wait_ge(consts_in, 32)
            transpose_rows(0, 0, 0)
            n = blocks(pe, body)
            transpose_hidden(2 * n)
            down(2 * n, 0, n)

        @block.vector
        def _(dve):
            def take_index(b, u):
                dve.wait_ge(xT_filled, 2 * b + 2)
                nc.vector.tensor_copy(index[:, u:u + 1], R["token_of"][:, bass.ds(b, 1)]).then_inc(index_ready, 1)

            def drain_rows(b, u):
                for half in range(2):
                    dve.wait_ge(xT_filled, 2 * b + half + 5)
                    gain = ffn_gain[:, 4 * half:4 * half + 4].unsqueeze(2).broadcast_to([P, 4, P])
                    nc.vector.tensor_tensor(xT[:, u, 4 * half:4 * half + 4, :], t_ps[half][:], gain, ALU.mult)\
                      .then_inc(xT_ready, 1)

            def drain_hidden(b):
                dve.wait_ge(hidden_filled, b + 1)
                nc.vector.tensor_copy(hiddenT[:], h_ps[:]).then_inc(hiddenT_ready, 1)

            def leave(b, u, r):
                dve.wait_ge(down_done, b + 3)
                dve.wait_ge(y_stored[u], 16 * r + 16)
                nc.vector.tensor_copy(y[:, u, 512:], y_ps[1][:]).then_inc(y_high, 1)

            for k, (s, by) in enumerate(((gate_done, 2), (up_done, 2), (down_done, 2), (xT_filled, 4), (hidden_ready, 1),
                                         (carried, 1), (hiddenT_ready, 1), (y_stored[0], 16), (y_stored[1], 16), (y_high, 1), (y_low, 1),
                                         (gate_in[0], 16), (gate_in[1], 16), (up_in[0], 16), (up_in[1], 16), (down_in[0], 16))):
                nc.vector.memset(lead[:, k:k + 1], 0.0).then_inc(s, by)

            def body(b, u, r, first):
                take_index(b + 2, u)
                if not first:
                    drain_hidden(b - 1)
                drain_rows(b + 1, 1 - u)
                dve.wait_ge(exp_ready, b + 1)
                nc.vector.tensor_scalar(sig[:], exp_g[:], 1.0, None, ALU.add).then_inc(sig_steps, 1)
                dve.wait_ge(sig_steps, 3 * b + 1)
                nc.vector.reciprocal(sig[:], sig[:]).then_inc(sig_steps, 1)
                dve.wait_ge(sig_steps, 3 * b + 2)
                nc.vector.tensor_tensor(sig[:], g_ps[u][:], sig[:], ALU.mult).then_inc(sig_steps, 1)
                dve.wait_ge(sig_steps, 3 * b + 3)
                dve.wait_ge(up_done, b + 3)
                nc.vector.tensor_tensor(hidden[:], u_ps[:], sig[:], ALU.mult).then_inc(hidden_ready, 1)
                if not first:
                    leave(b - 1, 1 - u, r - 1 + u)

            take_index(0, 0)
            take_index(1, 1)
            dve.wait_ge(consts_in, 32)
            drain_rows(0, 0)
            n = blocks(dve, body)
            drain_hidden(2 * n)
            leave(2 * n, 0, n)


def combine(nc, A, S, R):
    with ExitStack() as ctx:
        sb = lambda n, s, d=F32: ctx.enter_context(nc.sbuf_tensor(n, s, d))
        sem = semaphores(nc, ctx)
        gain = sb("final_gain", [P, D])
        index = sb("index7", [P, 2, 2], U32)
        part = [[sb(f"part{u}{k}", [P, D]) for k in range(2)] for u in range(2)]
        acc = sb("acc7", [P, 2, D])
        out = sb("out7", [P, 2, D])
        junk = sb("junk7", [P, D], BF16)
        square_sum, mean, guess, tmp, rstd = (sb(n, [P, 1]) for n in ("ssq7", "mean7", "guess7", "tmp7", "rstd7"))
        root = sb("root7", [P, 1])
        gain_in, carried = sem("gain_in"), sem("carried7")
        still, carrier = sb("still7", [1, 1]), sb("carrier7", [1, 1])
        res_in, out_stored = ([sem(f"{n}{u}") for u in range(2)] for n in ("res_in7", "out_stored7"))
        parts_in = [[sem(f"part_in{u}{k}") for k in range(2)] for u in range(2)]
        index_ready, added, summed, squared, mean_ready, rooted, guessed, steps, rstd_ready, scaled, out_ready = (
            sem(n + "7") for n in ("index_ready", "added", "summed", "squared", "mean_ready", "rooted", "guessed",
                                   "steps", "rstd_ready", "scaled", "out_ready"))
        block = ctx.enter_context(nc.Block())
        size = lambda n: NS if isinstance(n, int) and n == TILES else P

        @block.sync
        def _(sp):
            sp.dma_start(gain[:], A["norm_final_g"].unsqueeze(0).broadcast_to([P, D])).then_inc(gain_in, 16)

            def store(n, u):
                sp.wait_ge(out_ready, n + 1)
                if size(n) == NS:
                    sp.dma_start(A["y_sample"], out[0:NS, u, :]).then_inc(out_stored[u], 16)
                else:
                    sp.dma_start(A["y_prompt"][bass.ds(n * P, P), :], out[:, u, :]).then_inc(out_stored[u], 16)

            def body(n, u, r, past):
                if past == 2:
                    sp.wait_ge(out_ready, n - 1)
                m = size(n)
                sp.dma_start(acc[0:m, u, :], S["res"][bass.ds(n * P, m), :]).then_inc(res_in[u], 16)
                if past:
                    store(n - 1, 1 - u)

            tile_turns(sp, body)
            store(TILES, 0)
            sp.wait_ge(out_stored[0], 16 * (TILES // 2 + 1))
            sp.wait_ge(out_stored[1], 16 * (TILES // 2))

        @block.gpsimd
        def _(pool):
            def body(n, u, r, past):
                m = size(n)
                pool.wait_ge(index_ready, n + 1)
                if past == 2:
                    pool.wait_ge(summed, n - 1)
                if past:
                    pool.wait_ge(carried, n)
                nc.gpsimd.tensor_tensor(carrier[:], still[:], still[:], ALU.add).then_inc(carried, 1)
                for k in range(2):
                    pool.indirect_dma_start(out=part[u][k][0:m, :], out_offset=None, in_=S["y_slots"],
                                            in_offset=bass.IndirectOffsetOnAxis(ap=index[0:m, u, k:k + 1], axis=0))\
                        .then_inc(parts_in[u][k], 16)

            tile_turns(pool, body)

        @block.scalar
        def _(act):
            def body(n, u, r, past):
                m = size(n)
                act.wait_ge(summed, n + 1)
                if past:
                    act.wait_ge(rstd_ready, n)
                nc.scalar.activation(junk[0:m, :], acc[0:m, u, :], ACT.Square, accum_out=square_sum[0:m, :]).then_inc(squared, 1)
                act.wait_ge(mean_ready, n + 1)
                nc.scalar.activation(root[0:m, :], mean[0:m, :], ACT.Sqrt).then_inc(rooted, 1)
                act.wait_ge(rstd_ready, n + 1)
                if past == 2:
                    act.wait_ge(out_stored[u], 16 * r)
                nc.scalar.activation(out[0:m, u, :], acc[0:m, u, :], ACT.Copy, scale=rstd[0:m, :]).then_inc(scaled, 1)

            tile_turns(act, body)

        @block.vector
        def _(dve):
            def take_index(n, u):
                nc.vector.tensor_copy(index[:, u, :].unsqueeze(2), R["slots"][:, :, bass.ds(n, 1)]).then_inc(index_ready, 1)

            nc.vector.memset(still[:], 0.0)
            take_index(0, 0)
            dve.wait_ge(gain_in, 16)

            def body(n, u, r, past):
                m = size(n)
                if m == P:
                    take_index(n + 1, 1 - u)
                dve.wait_ge(res_in[u], 16 * r + 16)
                for k in range(2):
                    dve.wait_ge(parts_in[u][k], 16 * r + 16)
                    nc.vector.scalar_tensor_tensor(acc[0:m, u, :], part[u][k][0:m, :], R["gates"][0:m, bass.ds(n, 1), k],
                                                   acc[0:m, u, :], ALU.mult, ALU.add).then_inc(added if k == 0 else summed, 1)
                    if k == 0:
                        dve.wait_ge(added, n + 1)
                dve.wait_ge(squared, n + 1)
                nc.vector.tensor_scalar(mean[0:m, :], square_sum[0:m, :], 1.0 / D, EPS, ALU.mult, ALU.add).then_inc(mean_ready, 1)
                dve.wait_ge(rooted, n + 1)
                nc.vector.reciprocal(guess[0:m, :], root[0:m, :]).then_inc(guessed, 1)
                dve.wait_ge(guessed, n + 1)
                if past:
                    dve.wait_ge(scaled, n)
                refine_rsqrt(nc, dve, rstd[0:m, :], guess[0:m, :], mean[0:m, :], tmp[0:m, :], steps, 3 * n, rstd_ready)
                dve.wait_ge(scaled, n + 1)
                nc.vector.tensor_tensor(out[0:m, u, :], out[0:m, u, :], gain[0:m, :], ALU.mult).then_inc(out_ready, 1)

            tile_turns(dve, body)


SCRATCH = [("attqT", (PAIRS, P, SEQ), F32), ("attkT", (PAIRS, P, SEQ), F32), ("catT", (KT, P, SEQ), F32),
           ("sample", (NS, 8 * 512), F32), ("catT_sample", (P, KT, NS), F32),
           ("res", (ROWS, D), F32), ("hrows", (ROWS, D), F32),
           ("slot_token", (SLOT_BLOCKS * P, 1), I32), ("y_slots", (OUT_BLOCKS * P, D), F32)]


def build(nc, A, S):
    project_and_hgrn(nc, A, S)
    prompt_attention(nc, A, S)
    sample_mixer(nc, A, S)
    with ExitStack() as ctx:
        sb = lambda n, s, d: ctx.enter_context(nc.sbuf_tensor(n, s, d))
        R = {"chosen": [sb(f"chosen{k}", [P, NT, EXPERTS], F32) for k in range(2)],
             "gates": sb("gates", [P, NT, 2], F32), "slots": sb("slots", [P, 2, NT], U32),
             "block_expert": sb("block_expert", [1, P + 1], I32), "token_of": sb("token_of", [P, SLOT_BLOCKS], I32)}
        project_out_and_route(nc, A, S, R)
        with ExitStack() as of_experts:
            W = {n: of_experts.enter_context(nc.sbuf_tensor(f"w_{n}", shape, F32))
                 for n, shape in (("gate", [P, 2, KT, FF]), ("up", [P, 2, KT, FF]), ("down", [P, 2, FF // P, D]))}
            assign_slots(nc, A, S, R, W)
            experts(nc, A, S, R, W)
        combine(nc, A, S, R)

_INS = ['x_prompt', 'x_sample', 'cache_attn_k', 'cache_attn_v', 'state_hgrn', 'w_in', 'w_out', 'hg_lb_logits',
        'norm_final_g', 'w_route_group', 'w_route_expert',
        'w_expert_gate', 'w_expert_up', 'w_expert_down']
_OUTS = [('y_prompt', (SEQ, D)), ('y_sample', (NS, D)), ('new_k_prompt', (SEQ, ATW)), ('new_v_prompt', (SEQ, ATW)),
         ('new_hgrn_prompt', (HGH, HGD, HGD)), ('new_k_sample', (NS, WIN, ATW)), ('new_v_sample', (NS, WIN, ATW)),
         ('new_hgrn_sample', (NS, HGH, HGD, HGD))]
_SHAPES = [(1, SEQ, D), (NS, 1, D), (1, 1, SEQ, ATH, ATD), (1, 1, SEQ, ATH, ATD), (1, 1, HGH, HGD, HGD),
           (1, NS, WIN, ATH, ATD), (1, NS, WIN, ATH, ATD), (1, NS, HGH, HGD, HGD)]


def kernel(**inputs):
    import numpy as _np
    import concourse.bacc as _bacc
    from concourse import mybir as _mybir
    from concourse.bass_utils import run_bass_kernel_spmd as _run

    nc = _bacc.Bacc("TRN2", target_bir_lowering=False, num_devices=1)
    arrays, A = {}, {}
    given = {name: inputs[name] for name in _INS}
    for name, of in (("mix_gain", "norm_mix_g"), ("ffn_gain", "norm_ffn_g"), ("head_gain", "hg_norm_g")):
        given[name] = _np.asarray(inputs[of]).reshape(-1, P).T
    given.update(constants())
    given.update(attention_constants())
    given.update(sample_constants())
    given.update(routing_constants())
    for name, value in given.items():
        a = _np.ascontiguousarray(value)
        arrays[f"in_{name}_dram"] = a
        A[name] = nc.dram_tensor(f"in_{name}_dram", a.shape, _mybir.dt.from_np(a.dtype), kind="ExternalInput").ap()
    for name, shape in _OUTS:
        A[name] = nc.dram_tensor(f"out_{name}_dram", shape, F32, kind="ExternalOutput").ap()
    S = {name: nc.dram_tensor(f"scratch_{name}", shape, dt, kind="Internal").ap() for name, shape, dt in SCRATCH}
    build(nc, A, S)
    r = _run(nc, [arrays], core_ids=[0])
    return tuple(r.results[0][f"out_{name}_dram"].reshape(shape) for (name, _), shape in zip(_OUTS, _SHAPES))
```
